# Optimizing a Trainium2 kernel written in Bass

```python
import math
import jax, jax.numpy as jnp
from jax import lax
import numpy as np

D_MODEL = 2048
BATCH = 1
SEQ = 512
DEPTH = 1
DEC_BATCH = 8
DEC_SEQ = 4
PAST_LEN = 4096
PAGE_SIZE = 128

D_MIX = D_MODEL
D_GLA = D_MIX // 2
GLA_HEADS = 4
GLA_DK = D_GLA // 2 // GLA_HEADS
GLA_DV = D_GLA // GLA_HEADS
GLA_RANK = 16
GLA_TAU = 16.0
GLA_CHUNK = 64
D_CONV = D_MIX // 4
CONV_W = 3
D_CM = D_MIX // 4
CM_HEADS = 4
CM_HD = D_CM // CM_HEADS
CM_CHUNK = 128
D_FF = ((8 * D_MODEL + 3 * 256 - 1) // (3 * 256)) * 256
EPS = 1e-6
IN_SIZES = (GLA_HEADS * GLA_DK, GLA_HEADS * GLA_DK, D_GLA, D_GLA, GLA_RANK,
            D_CONV, D_CONV, D_CONV, D_CM, D_CM)
D_IN = sum(IN_SIZES)

kernel_name = "hybrid_gla_shortconv_chunkmlp_step"

def _split_idx():
    idx, acc = [], 0
    for s in IN_SIZES[:-1]:
        acc += s
        idx.append(acc)
    return idx

def rmsnorm(x, g):
    xf = x.astype(jnp.float32)
    y = xf * lax.rsqrt(jnp.mean(xf * xf, axis=-1, keepdims=True) + EPS)
    return (y * g.astype(jnp.float32)).astype(x.dtype)

def layernorm(x, g, b):
    xf = x.astype(jnp.float32)
    mu = jnp.mean(xf, axis=-1, keepdims=True)
    xc = xf - mu
    y = xc * lax.rsqrt(jnp.mean(xc * xc, axis=-1, keepdims=True) + EPS)
    return (y * g.astype(jnp.float32) + b.astype(jnp.float32)).astype(x.dtype)

def gla_chunked(q, k, v, loga, S0):
    B, L = q.shape[0], q.shape[1]
    C = math.gcd(L, GLA_CHUNK)
    N = L // C

    def blk(t):
        return t.reshape(B, N, C, GLA_HEADS, t.shape[-1]).transpose(0, 3, 1, 2, 4).astype(jnp.float32)

    qb, kb, vb, ab = blk(q), blk(k), blk(v), blk(loga)
    b = jnp.cumsum(ab, axis=3)
    g = b[:, :, :, -1]
    qt = qb * jnp.exp(b)
    kt = kb * jnp.exp(-b)
    kd = kb * jnp.exp(g[:, :, :, None] - b)
    mask = jnp.tril(jnp.ones((C, C), dtype=bool))
    A = jnp.where(mask, jnp.einsum('bhncd,bhnsd->bhncs', qt, kt), 0.0)
    o_intra = jnp.einsum('bhncs,bhnse->bhnce', A, vb)
    dS = jnp.einsum('bhncd,bhnce->bhnde', kd, vb)

    def step(S, inp):
        g_n, dS_n = inp
        return jnp.exp(g_n)[..., None] * S + dS_n, S

    S_fin, S_prev = lax.scan(step, S0.astype(jnp.float32),
                             (jnp.moveaxis(g, 2, 0), jnp.moveaxis(dS, 2, 0)))
    S_prev = jnp.moveaxis(S_prev, 0, 2)
    o = o_intra + jnp.einsum('bhncd,bhnde->bhnce', qt, S_prev)
    o = o.transpose(0, 2, 3, 1, 4).reshape(B, L, GLA_HEADS, GLA_DV)
    return o, S_fin.astype(S0.dtype)

def mixer(xn, S0, conv_buf, w_in, w_a2, b_a, gla_g, conv_w, conv_b, cm_ln_g, cm_ln_b, cm_ws, cm_bs, w_out):
    B, L, _ = xn.shape
    proj = xn @ w_in
    q, k, v, r, a_lr, cb, cc, ch, cu, cv = jnp.split(proj, _split_idx(), axis=-1)

    loga = jax.nn.log_sigmoid((a_lr @ w_a2 + b_a).astype(jnp.float32)) / GLA_TAU
    o, S_new = gla_chunked((q * (GLA_DK ** -0.5)).reshape(B, L, GLA_HEADS, GLA_DK),
                           k.reshape(B, L, GLA_HEADS, GLA_DK),
                           v.reshape(B, L, GLA_HEADS, GLA_DV),
                           loga.reshape(B, L, GLA_HEADS, GLA_DK), S0)
    o = o * lax.rsqrt(jnp.mean(o * o, axis=-1, keepdims=True) + EPS)
    o = o * gla_g.reshape(GLA_HEADS, GLA_DV).astype(jnp.float32)
    o_gla = o.reshape(B, L, D_GLA).astype(xn.dtype) * jax.nn.silu(r)

    z = cc * ch
    zp = jnp.concatenate([conv_buf.astype(z.dtype), z], axis=1)
    conv = conv_b
    for j in range(CONV_W):
        conv = conv + conv_w[j] * zp[:, j:j + L]
    o_conv = cb * conv
    conv_new = zp[:, L:]

    u = jax.nn.gelu(cu, approximate=False)
    vv = layernorm(jax.nn.gelu(cv, approximate=False), cm_ln_g, cm_ln_b)
    T = min(L, CM_CHUNK)
    N = L // T
    vb = vv.reshape(B, N, T, CM_HEADS, CM_HD)
    Wm = jnp.where(jnp.tril(jnp.ones((T, T), dtype=bool)), cm_ws[:, :T, :T], 0.0)
    zc = jnp.einsum('hts,bnshc->bnthc', Wm, vb) + jnp.transpose(cm_bs[:, :T])[None, None, :, :, None]
    o_cm = u * zc.reshape(B, L, D_CM)

    out = jnp.concatenate([o_gla, o_conv, o_cm], axis=-1) @ w_out
    return out, S_new, conv_new, vv

def swiglu(x, w_gate, w_up, w_down):
    return (jax.nn.silu(x @ w_gate) * (x @ w_up)) @ w_down

def setup_inputs(seed: int = 0) -> dict:
    key = jax.random.key(seed)
    ks = jax.random.split(key, 24)
    nrm = lambda k, s: jax.random.normal(k, s, dtype=jnp.float32)
    return {
        "x_prompt": nrm(ks[0], (BATCH, SEQ, D_MODEL)),
        "x_sample": nrm(ks[1], (DEC_BATCH, DEC_SEQ, D_MODEL)),
        "state_gla": nrm(ks[2], (DEPTH, DEC_BATCH, GLA_HEADS, GLA_DK, GLA_DV)),
        "state_conv": nrm(ks[3], (DEPTH, DEC_BATCH, CONV_W - 1, D_CONV)),
        "norm1_g": 1.0 + 0.05 * nrm(ks[4], (DEPTH, D_MODEL)),
        "w_in": nrm(ks[5], (DEPTH, D_MODEL, D_IN)) * D_MODEL ** -0.5,
        "w_a2": nrm(ks[6], (DEPTH, GLA_RANK, GLA_HEADS * GLA_DK)) * GLA_RANK ** -0.5,
        "b_a": 0.1 * nrm(ks[7], (DEPTH, GLA_HEADS * GLA_DK)),
        "gla_g": 1.0 + 0.05 * nrm(ks[8], (DEPTH, D_GLA)),
        "conv_w": nrm(ks[9], (DEPTH, CONV_W, D_CONV)) * CONV_W ** -0.5,
        "conv_b": 0.01 * nrm(ks[10], (DEPTH, D_CONV)),
        "cm_ln_g": 1.0 + 0.05 * nrm(ks[11], (DEPTH, D_CM)),
        "cm_ln_b": 0.01 * nrm(ks[12], (DEPTH, D_CM)),
        "cm_ws": 0.1 * nrm(ks[13], (DEPTH, CM_HEADS, CM_CHUNK, CM_CHUNK)),
        "cm_bs": 1.0 + 0.1 * nrm(ks[14], (DEPTH, CM_HEADS, CM_CHUNK)),
        "w_out": nrm(ks[15], (DEPTH, D_MIX, D_MODEL)) * D_MIX ** -0.5,
        "norm2_g": 1.0 + 0.05 * nrm(ks[16], (DEPTH, D_MODEL)),
        "w_gate": nrm(ks[17], (DEPTH, D_MODEL, D_FF)) * D_MODEL ** -0.5,
        "w_up": nrm(ks[18], (DEPTH, D_MODEL, D_FF)) * D_MODEL ** -0.5,
        "w_down": nrm(ks[19], (DEPTH, D_FF, D_MODEL)) * D_FF ** -0.5,
        "final_g": 1.0 + 0.05 * nrm(ks[20], (D_MODEL,)),
    }

def reference(x_prompt, x_sample, state_gla, state_conv, norm1_g, w_in, w_a2, b_a, gla_g, conv_w, conv_b,
              cm_ln_g, cm_ln_b, cm_ws, cm_bs, w_out, norm2_g, w_gate, w_up, w_down, final_g):
    xp, xs = x_prompt, x_sample
    S0p = jnp.zeros((BATCH, GLA_HEADS, GLA_DK, GLA_DV), dtype=x_prompt.dtype)
    cbp = jnp.zeros((BATCH, CONV_W - 1, D_CONV), dtype=x_prompt.dtype)
    gla_p, conv_p, gla_s, conv_s, cmv_s = [], [], [], [], []
    for l in range(DEPTH):
        lw = (w_in[l], w_a2[l], b_a[l], gla_g[l], conv_w[l], conv_b[l], cm_ln_g[l], cm_ln_b[l],
              cm_ws[l], cm_bs[l], w_out[l])
        hp, Sp, cp, _ = mixer(rmsnorm(xp, norm1_g[l]), S0p, cbp, *lw)
        xp = xp + hp
        xp = xp + swiglu(rmsnorm(xp, norm2_g[l]), w_gate[l], w_up[l], w_down[l])
        hs, Ss, cs, vs = mixer(rmsnorm(xs, norm1_g[l]), state_gla[l], state_conv[l], *lw)
        xs = xs + hs
        xs = xs + swiglu(rmsnorm(xs, norm2_g[l]), w_gate[l], w_up[l], w_down[l])
        gla_p.append(Sp); conv_p.append(cp)
        gla_s.append(Ss); conv_s.append(cs); cmv_s.append(vs)
    y_prompt = rmsnorm(xp, final_g)
    y_sample = rmsnorm(xs, final_g)
    return (y_prompt, y_sample, jnp.stack(gla_p), jnp.stack(conv_p), jnp.stack(gla_s), jnp.stack(conv_s), jnp.stack(cmv_s))


_drawn_inputs = setup_inputs


def setup_inputs(seed=0):
    import zlib

    import numpy as np

    out = dict(_drawn_inputs(seed))
    spreads = {}
    factors = {'gla_g': 3.239, 'conv_b': 8.0, 'cm_ln_b': 5.759, 'cm_bs': 3.194, 'norm2_g': 2.826}
    for name, (base, spread) in spreads.items():
        noise = np.random.default_rng([zlib.crc32(name.encode()), seed]).standard_normal(out[name].shape)
        drawn = base * np.exp(spread * noise) if base else spread * noise
        out[name] = __import__('jax').numpy.asarray(drawn.astype(out[name].dtype))
    for name, factor in factors.items():
        out[name] = (out[name] * factor).astype(out[name].dtype)
    return out
```

```python
from contextlib import ExitStack

import concourse.bass as bass
from concourse import mybir

F32 = mybir.dt.float32
F32R = mybir.dt.float32r
I32 = mybir.dt.int32
ALU = mybir.AluOpType
ACT = mybir.ActivationFunctionType

P = 128
D = 2048
KT = D // P
TP = 512
DB, DS = 8, 4
TS = DB * DS
T = TP + TS
TH = T // 2
HEADS, DK, DV, RANK = 4, 128, 256, 16
CHUNK = 64
NCHUNK = TP // CHUNK
CMC = 128
DFF = 5632
FT = DFF // P
GROUPS = 4
FG = FT // GROUPS
EPS = 1e-6

T_Q, T_K, T_CV, T_CU, T_V, T_CONV, T_R, N_IN = 1, 5, 9, 13, 17, 25, 37, 45
HK = KT // 2
CH = HK * P
RING = 4
RAW = 2
C_OUT = 2 * N_IN
C_FF = C_OUT + 2 * KT
C_GU = 4 * FG
C_GRP = C_GU + 2 * KT
C_END = C_FF + GROUPS * C_GRP
DA = (FG + 1) // 2
MIX_ORDER = list(range(HK, KT)) + list(range(HK))

VAR1_AT = 3
Z_AT = (5, 7)
B_AT = (19, 21, 23, 25, 27)
KDT_AT = 29
MU_AT, VAR_CM_AT, VVT_AT, ZC_AT = 27, 29, 31, (33, 35)
VT_AT = tuple(36 + 2 * i for i in range(8))
P_AT = tuple(51 + 2 * n for n in range(NCHUNK + 1))
S_AT = tuple(50 + 2 * i for i in range(10))
OSQ_AT = 69
ON_AT = (71, 73, 75, 77)

V_G1, V_G2, V_GF, V_GLA, V_CW, V_CB, V_LG, V_LB, NV = 0, 16, 32, 48, 56, 68, 72, 76, 80


A_KINDS = ("var1", "z", "b", "mu", "var_cm", "vvt", "p", "s", "on")
V_KINDS = A_KINDS + ("kdt", "zc", "vt")


def mixer_plan():
    plan = {}
    for kind, places in (("var1", (VAR1_AT,)), ("z", Z_AT), ("b", B_AT), ("kdt", (KDT_AT,)), ("mu", (MU_AT,)),
                         ("var_cm", (VAR_CM_AT,)), ("vvt", (VVT_AT,)), ("zc", ZC_AT), ("vt", VT_AT), ("p", P_AT),
                         ("s", S_AT), ("on", ON_AT)):
        for i, c in enumerate(places):
            plan.setdefault(c, []).append((kind, i))
    order = [piece for c in sorted(plan) for piece in plan[c]]
    return plan, order


class Count:

    def __init__(self):
        self.n = 0

    def up(self):
        self.n += 1
        return self.n


def build(nc, xT, w_alr, w_in, w_out, w_gu, w_da, w_db, vecs, wa2, wm, wsbd, bs, s0, cbuf, ident, tri, maskA, maskS,
          bmask, yT, gla_p, gla_s, conv_o, cmv):
    with ExitStack() as ctx:
        def sb(name, shape, dt=F32):
            return ctx.enter_context(nc.sbuf_tensor(name, shape, dt))

        def sem(name):
            return ctx.enter_context(nc.semaphore(name))

        trunk = sb("trunk", [P, KT, T])
        op_hi = sb("op_hi", [P, KT, T], F32R)
        op_lo = sb("op_lo", [P, KT, T], F32R)
        w_raw = sb("w_raw", [P, RAW, CH])
        w_hi = sb("w_hi", [P, RING, CH], F32R)
        w_lo = sb("w_lo", [P, RING, CH], F32R)
        vec = sb("vec", [P, NV])
        idn = sb("idn", [P, P])
        onesf = sb("onesf", [P, P])
        rstd = sb("rstd", [P, T])
        tmp = sb("tmp", [P, 2, T])
        cst = sb("cst", [P, 4, 2 + 2 * DB])
        with ExitStack() as ff:
            hid_hi = ff.enter_context(nc.sbuf_tensor("hid_hi", [P, FG, T], F32R))
            hid_lo = ff.enter_context(nc.sbuf_tensor("hid_lo", [P, FG, T], F32R))
        mix = sb("mix", [P, KT, T])
        kd = sb("kd", [P, 4, HEADS * DK])
        vs = sb("vs", [64, HEADS * DV])
        S = sb("S", [P, HEADS, DV])
        with nc.sbuf_tensor("alw", [P, KT, P], F32R) as alw:
            pass
        S0 = sb("S0", [P, 2, 4 * DV])
        kdm = sb("kdm", [32, 4, DK])
        AT = sb("AT", [P, HEADS * CHUNK])
        ATs = sb("ATs", [32, HEADS * TS])
        triu = sb("triu", [P, P + TS])
        mA = sb("mA", [P, HEADS * CHUNK], I32)
        mS = sb("mS", [32, HEADS * TS], I32)
        bm = sb("bm", [64, DB])
        egp = sb("egp", [P, NCHUNK, HEADS])
        egs = sb("egs", [P, HEADS, DB])
        vvts = sb("vvts", [32, 4 * P])
        wsb = sb("wsb", [32, 4, TS])
        zp = sb("zp", [P, 2 + TP + DB * (2 + DS)])
        cbs = sb("cbs", [P, 4, 2 * DB])
        trf = trunk[:].rearrange("p k t -> p (k t)")
        qT = trf[:, 0:HEADS * T].rearrange("p (h t) -> p h t", h=HEADS)
        kT = trf[:, HEADS * T:2 * HEADS * T].rearrange("p (h t) -> p h t", h=HEADS)
        v = trf[:, 2 * HEADS * T:2 * HEADS * T + 4 * HEADS * DV].rearrange("p (j e) -> p j e", j=4)
        mxf = mix[:].rearrange("p k t -> p (k t)")
        loga = mxf[:, 0:5 * 512].rearrange("p (j d) -> p j d", j=5)
        ex_g, ex_p, ex_n = (mxf[:, (5 + i) * 512:(6 + i) * 512] for i in range(3))
        vvt = S0[:].rearrange("p a (b c) -> p (a b) c", b=2)
        wmm = S[:].rearrange("p h e -> p (h e)")[:, 0:512]
        bsb = S[:].rearrange("p h e -> p (h e)")[:, 512:1024]
        kdf = kd[:].rearrange("p j d -> p (j d)")
        alr = kdf[0:2 * RANK + 1, 0:T]
        wa2s = kdf[0:2 * RANK + 1, T:T + HEADS * DK]
        lnb = zp[:, 2:2 + T]
        osq = kdf[:, 0:2 * T].rearrange("p (a t) -> p a t", a=2)
        orstd = kdf[:, 2 * T:3 * T]
        al_raw = tmp[:].rearrange("p a t -> p (a t)")[:, 0:KT * RANK]
        acc = [ctx.enter_context(nc.psum_tensor(f"acc{i}", [P, 2, 512], F32)) for i in range(2)]
        g01 = ctx.enter_context(nc.psum_tensor("g01", [P, 2, 512], F32))
        g23 = ctx.enter_context(nc.psum_tensor("g23", [P, 2, 512], F32))
        g = [g01[:, 0, :], g01[:, 1, :], g23[:, 0, :], g23[:, 1, :]]

        def accv(t):
            return acc[t % 2][:, :, 0:TH]

        def two(ap):
            return ap.rearrange("p (a t) -> p a t", a=2)

        consts_in = sem("consts_in")
        alr_w_in = sem("alr_w_in")
        mid_in = sem("mid_in")
        x_in = [sem(f"x_in{i}") for i in range(8)]
        w_landed = [sem(f"w_landed{i}") for i in range(RAW)]
        hi_ready = sem("hi_ready")
        lo_ready = sem("lo_ready")
        zeroed = sem("zeroed")
        alr_hi = sem("alr_hi")
        alr_w = sem("alr_w")
        op_h = sem("op_h")
        op_rdy = sem("op_rdy")
        sq_done = sem("sq_done")
        sq_add = sem("sq_add")
        chunk_done = sem("chunk_done")
        acc_free = sem("acc_free")
        inter = sem("inter")
        post_v = sem("post_v")
        post_a = sem("post_a")
        v_to_a = sem("v_to_a")
        a_to_v = sem("a_to_v")
        v_own = sem("v_own")
        a_own = sem("a_own")
        gelu_done = sem("gelu_done")
        cm_sq = sem("cm_sq")
        cm_add = sem("cm_add")
        cmv_out = sem("cmv_out")
        silu_r = sem("silu_r")
        osq_a = sem("osq_a")
        osq_rdy = sem("osq_rdy")
        mix_done = sem("mix_done")
        s0_in = [sem(f"s0_in{i}") for i in range(2)]
        s0_out = [sem(f"s0_out{i}") for i in range(2)]
        x_back = sem("x_back")
        h_done = sem("h_done")
        hsq_done = sem("hsq_done")
        hsq_add = sem("hsq_add")
        var_done = sem("var_done")
        std_done = sem("std_done")
        rstd_ok = sem("rstd_ok")
        gate_act = sem("gate_act")
        hid_f = sem("hid_f")
        hid_h = sem("hid_h")
        hid_rdy = sem("hid_rdy")
        out_rdy = sem("out_rdy")
        stored = sem("stored")

        plan, order = mixer_plan()

        def number(piece):
            return order.index(piece) + 1

        def parts(kinds, piece):
            return sum(p[0] in kinds for p in order[:number(piece)])

        def landed(c, slot):
            return c * 8 - 8 * (slot % RAW)

        def osl(k):
            return MIX_ORDER[k]

        block = ctx.enter_context(nc.Block())

        @block.sync
        def _(sp):
            def load(slot, src, c, cols=CH):
                if not isinstance(c, int) or c >= 4:
                    sp.wait_ge(hi_ready, c - 3)
                    sp.wait_ge(lo_ready, c - 3)
                sp.dma_start(w_raw[:, slot % RAW, 0:cols], src).then_inc(w_landed[slot % RAW], 16)

            def load_x(i):
                sp.dma_start(trunk[:, 2 * i:2 * i + 2, :], xT[:, 2 * i:2 * i + 2, :]).then_inc(x_in[i], 16)

            sp.dma_start(vec[:], vecs).then_inc(consts_in, 16)
            sp.dma_start(al_raw, w_alr.rearrange("p k m -> p (k m)")).then_inc(alr_w_in, 16)
            load_x(0)
            load(2, w_in[0], 2)
            load_x(1)
            load(3, w_in[1], 3)
            for i in range(2, 8):
                load_x(i)
            for dst, src in ((idn[:], ident), (triu[:], tri), (mA[:], maskA), (mS[:], maskS), (bm[32:64, :], bmask),
                             (wa2s, wa2), (wmm, wm), (wsb[:], wsbd), (bsb, bs.partition_broadcast(P)),
                             (cbs[:], cbuf)):
                sp.dma_start(dst, src).then_inc(mid_in, 16)

            def s0_dram(t, i):
                return t[i // 2, i % 2]

            def store_s0(i):
                sp.wait_ge(post_v, parts(V_KINDS, ("s", i + 2)))
                sp.dma_start(s0_dram(gla_s, i), S0[:, i % 2, :]).then_inc(s0_out[i % 2], 16)

            def load_s0(i):
                if i >= 2:
                    sp.wait_ge(s0_out[i % 2], 16 * (i // 2))
                else:
                    sp.wait_ge(inter, number(("zc", 1)))
                sp.dma_start(S0[:, i % 2, :], s0_dram(s0, i)).then_inc(s0_in[i % 2], 16)

            for c in range(4, C_OUT):
                if c == ZC_AT[1] + 8:
                    load_s0(0)
                    load_s0(1)
                for i in range(8):
                    if c == S_AT[2 + i] + 7:
                        store_s0(i)
                    if c == S_AT[2 + i] + 8 and i + 2 < 8:
                        load_s0(i + 2)
                if c == S_AT[-1] + 8:
                    sp.wait_ge(post_v, parts(V_KINDS, ("p", NCHUNK)))
                    sp.dma_start(gla_p.rearrange("h d e -> d h e"), S[:]).then_inc(stored, 16)
                    sp.wait_ge(inter, number(("s", 9)))
                    for i in range(4):
                        sp.dma_start(trunk[:, 4 * i:4 * i + 4, :], xT[:, 4 * i:4 * i + 4, :]).then_inc(x_back, 16)
                load(c, w_in[c - 2], c)
            with sp.Fori(0, KT // 2) as i:
                for s in range(4):
                    load(C_OUT + s, w_out[i * 4 + s], i * 4 + (C_OUT + s))
            sp.wait_ge(mix_done, 8)
            sp.dma_start(conv_o, cst[:]).then_inc(stored, 16)
            with sp.Fori(0, GROUPS) as gr:
                with sp.Fori(0, FG) as f:
                    for s in range(4):
                        load(C_FF + s, w_gu[gr * C_GU + f * 4 + s], gr * C_GRP + f * 4 + (C_FF + s))
                with sp.Fori(0, KT // 2) as i:
                    for s in range(4):
                        m = gr * KT + i * 2 + s // 2
                        src, cols = (w_db[m], (FG - DA) * P) if s % 2 else (w_da[m], DA * P)
                        load(C_FF + s, src, gr * C_GRP + i * 4 + (C_FF + C_GU + s), cols)
            for i in range(8):
                sp.wait_ge(out_rdy, 2 * i + 2)
                sp.dma_start(yT[:, 2 * i:2 * i + 2, :], trunk[:, 2 * i:2 * i + 2, :]).then_inc(stored, 16)
            sp.wait_ge(stored, 16 * (1 + 1 + 8))
            sp.wait_ge(cmv_out, 16)
            sp.wait_ge(s0_out[0], 16 * 4)
            sp.wait_ge(s0_out[1], 16 * 4)

        @block.gpsimd
        def _(pool):
            nc.gpsimd.memset(alw[:].bitcast(F32), 0.0).then_inc(zeroed, 1)
            nc.gpsimd.memset(onesf[:], 1.0).then_inc(zeroed, 1)
            nc.gpsimd.memset(AT[:], 0.0).then_inc(zeroed, 1)
            nc.gpsimd.memset(ATs[:], 0.0).then_inc(zeroed, 1)
            pool.wait_ge(zeroed, 4)
            nc.gpsimd.memset(alr[2 * RANK:2 * RANK + 1, :], 1.0).then_inc(zeroed, 1)
            pool.wait_ge(zeroed, 5)
            nc.gpsimd.memset(zp[:, 0:2], 0.0).then_inc(zeroed, 1)
            pool.wait_ge(zeroed, 6)
            pool.wait_ge(mid_in, 16 * 10)
            w3 = wmm.rearrange("p (h t) -> p h t", h=4)
            nc.gpsimd.affine_select(out=w3, in_=w3, compare_op=ALU.is_ge, fill=0.0, base=0,
                                    pattern=[[0, 4], [1, P]], channel_multiplier=-1).then_inc(zeroed, 1)
            pool.wait_ge(zeroed, 7)
            nc.gpsimd.affine_select(out=wsb[:], in_=wsb[:], compare_op=ALU.is_ge, fill=0.0, base=0,
                                    pattern=[[0, 4], [1, TS]], channel_multiplier=-1).then_inc(zeroed, 1)

        @block.scalar
        def _(act):
            own, took = Count(), Count()

            def chain(ins):
                ins.then_inc(a_own, 1)
                act.wait_ge(a_own, own.up())

            def take():
                act.wait_ge(v_to_a, took.up())

            def split_hi(c, slot):
                act.wait_ge(w_landed[slot % RAW], landed(c, slot))
                if not isinstance(c, int) or c >= 6:
                    act.wait_ge(chunk_done, c - 3)
                nc.scalar.copy(w_hi[:, slot % RING, :], w_raw[:, slot % RAW, :]).then_inc(hi_ready, 1)

            act.wait_ge(consts_in, 16)
            act.wait_ge(alr_w_in, 16)
            act.wait_ge(zeroed, 1)
            nc.scalar.copy(alw[:, :, 0:RANK], al_raw.rearrange("p (k m) -> p k m", k=KT)).then_inc(alr_hi, 1)
            for k in range(KT):
                act.wait_ge(x_in[k // 2], 16)
                nc.scalar.mul(op_hi[:, k, :], trunk[:, k, :], vec[:, V_G1 + k:V_G1 + k + 1]).then_inc(op_h, 1)
                if k == 0:
                    act.wait_ge(alr_w, 1)
                if k >= 2:
                    act.wait_ge(sq_add, k - 1)
                nc.scalar.activation(tmp[:, k % 2, :], trunk[:, k, :], ACT.Square).then_inc(sq_done, 1)
                if k in (1, 3, 8, 12):
                    c = {1: 2, 3: 3, 8: 4, 12: 5}[k]
                    split_hi(c, c)

            def silu(i):
                take()
                nc.scalar.activation(tmp[:, i % 2, :], tmp[:, i % 2, :], ACT.Silu).then_inc(silu_r, 1)

            def out_squares(h):
                for e in range(2):
                    nc.scalar.activation(osq[:, e, :], mix[:, 2 * h + e, :], ACT.Square).then_inc(osq_a, 1)

            def post(kind, i):
                act.wait_ge(inter, number((kind, i)))
                last = None
                if kind == "var1":
                    last = nc.scalar.activation(two(rstd[:]), g01[:, :, 0:TH], ACT.Sqrt, bias=EPS, scale=1.0 / D)
                elif kind == "z":
                    for j in (range(4) if i == 0 else (4,)):
                        rows = P if j < 4 else TS
                        lj = loga[0:rows, j, :]
                        chain(nc.scalar.activation(lj, g[j % 4][0:rows, :], ACT.Abs))
                        chain(nc.scalar.activation(lj, lj, ACT.Exp, scale=-1.0))
                        last = nc.scalar.activation(lj, lj, ACT.Ln, bias=1.0)
                        if j < 3:
                            last.then_inc(a_to_v, 1)
                elif kind == "b":
                    w = 4 * (P if i < 4 else TS)
                    nc.scalar.activation(ex_p[:, 0:w], g[0][:, 0:w], ACT.Exp).then_inc(a_to_v, 1)
                    nc.scalar.activation(ex_n[:, 0:w], g[0][:, 0:w], ACT.Exp, scale=-1.0).then_inc(a_to_v, 1)
                    take()
                    last = nc.scalar.activation(ex_g[:, 0:w], ex_g[:, 0:w], ACT.Exp)
                elif kind == "mu":
                    for h in range(4):
                        take()
                        if h >= 2:
                            act.wait_ge(cm_add, h - 1)
                        last = nc.scalar.activation(tmp[:, h % 2, :], mix[:, 12 + h, :], ACT.Square)
                        if h < 3:
                            last.then_inc(cm_sq, 1)
                elif kind == "var_cm":
                    last = nc.scalar.activation(two(lnb), g23[:, :, 0:TH], ACT.Sqrt, bias=EPS, scale=1.0 / (4 * P))
                elif kind == "vvt":
                    act.wait_ge(post_v, parts(V_KINDS, ("var_cm", 0)))
                    act.dma_start(cmv, mix[:, 12:16, TP:T]).then_inc(cmv_out, 16)
                    nc.scalar.copy(vvt[:, 2, :], g[2])
                    last = nc.scalar.copy(vvt[:, 3, :], g[3])
                elif kind == "p":
                    if i >= 1:
                        last = nc.scalar.copy(mix[:, 0:8, CHUNK * (i - 1):CHUNK * i],
                                              g[1].rearrange("p (s t) -> p s t", s=8))
                elif kind == "s":
                    if i == 1:
                        last = nc.scalar.copy(mix[:, 0:8, TP:T], g[0][:, 0:8 * TS].rearrange("p (s t) -> p s t", s=8))
                elif kind == "on":
                    last = nc.scalar.activation(two(orstd), g01[:, :, 0:TH], ACT.Sqrt, bias=EPS, scale=1.0 / DV)
                if last is None:
                    last = act.nop()
                last.then_inc(post_a, 1)
                if kind == "on" and i < 3:
                    out_squares(i + 1)

            def evac(t):
                if T_CV <= t < T_V:
                    j = t - T_CV
                    take()
                    m = mix[:, 12 + j if t < T_CU else 4 + j, :]
                    nc.scalar.activation(m, m, ACT.Gelu).then_inc(gelu_done, 1)
                elif t >= T_R:
                    silu(t - T_R)

            def op_hi_tile(k):
                act.wait_ge(mix_done, 8 if k < 8 else k + 1)
                nc.scalar.copy(op_hi[:, k, :], mix[:, osl(k), :]).then_inc(op_h, 1)

            for c in range(2, C_OUT):
                act.wait_ge(chunk_done, c + 1)
                if c == C_OUT - 1:
                    split_hi(c + 4, c + 4)
                    for k in range(8):
                        op_hi_tile(k)
                    evac(c // 2)
                    for k in range(8, KT):
                        op_hi_tile(k)
                    continue
                if c % 2 and c > 3:
                    evac(c // 2)
                for kind, i in plan.get(c, ()):
                    if kind in A_KINDS:
                        post(kind, i)
                if c == OSQ_AT:
                    act.wait_ge(post_v, parts(V_KINDS, ("s", 9)))
                    act.wait_ge(post_v, parts(V_KINDS, ("p", NCHUNK)))
                    out_squares(0)
                split_hi(c + 4, c + 4)

            def square_h(m, par, base):
                act.wait_ge(hsq_add, m + (base[1] - 1))
                act.wait_ge(h_done, m + (base[0] + 1))
                nc.scalar.activation(tmp[:, par, :], trunk[:, m, :], ACT.Square).then_inc(hsq_done, 1)

            def sqrt_var(n):
                act.wait_ge(var_done, n)
                nc.scalar.activation(two(rstd[:]), g01[:, :, 0:TH], ACT.Sqrt, bias=EPS, scale=1.0 / D)\
                    .then_inc(std_done, 1)

            with act.Fori(0, KT // 2) as i:
                for s in range(4):
                    c = i * 4 + (C_OUT + s)
                    act.wait_ge(chunk_done, c + 1)
                    if s % 2:
                        square_h(i * 2 + s // 2, s // 2, (0, 2))
                    split_hi(c + 4, C_OUT + s + 4)
            act.wait_ge(chunk_done, C_FF)
            for k in range(KT):
                act.wait_ge(h_done, k + 1)
                nc.scalar.mul(op_hi[:, k, :], trunk[:, k, :], vec[:, V_G2 + k:V_G2 + k + 1]).then_inc(op_h, 1)
            sqrt_var(1)

            def group(gr, last):
                with act.Fori(0, FG) as f:
                    for s in range(4):
                        c = gr * C_GRP + f * 4 + (C_FF + s)
                        act.wait_ge(chunk_done, c + 1)
                        if s == 1:
                            act.wait_ge(acc_free, gr * (C_GRP // 2) + f * 2 + (C_FF // 2 + 1))
                            nc.scalar.activation(tmp[:, 1, :], tmp[:, 1, :], ACT.Silu).then_inc(gate_act, 1)
                        if s == 3:
                            act.wait_ge(hid_f, gr * FG + f + 1)
                            nc.scalar.copy(hid_hi[:, f, :], tmp[:, 0, :]).then_inc(hid_h, 1)
                        split_hi(c + 4, C_FF + s + 4)

                def down(i, tail):
                    for s in range(4):
                        c = gr * C_GRP + i * 4 + (C_FF + C_GU + s)
                        act.wait_ge(chunk_done, c + 1)
                        if last and s % 2:
                            square_h(i * 2 + s // 2, s // 2, (KT, 20))
                        if not tail:
                            split_hi(c + 4, C_FF + s + 4)

                with act.Fori(0, KT // 2 - (1 if last else 0)) as i:
                    down(i, False)
                if last:
                    down(KT // 2 - 1, True)

            with act.Fori(0, GROUPS - 1) as gr:
                group(gr, False)
            group(GROUPS - 1, True)
            sqrt_var(2)

        @block.tensor
        def _(pe):
            def products(t, slot, j, k, start, stop, rhs_hi, rhs_lo):
                w_h = w_hi[:, slot % RING, j * P:(j + 1) * P]
                w_l = w_lo[:, slot % RING, j * P:(j + 1) * P]
                for n, (w, x) in enumerate(((w_h, rhs_hi), (w_h, rhs_lo), (w_l, rhs_hi))):
                    for a in range(2):
                        last = nc.tensor.matmul(acc[t % 2][:, a, 0:TH], w, x[:, k, a * TH:(a + 1) * TH],
                                                start=start and n == 0, stop=stop and n == 2)
                return last

            def chunk(c, slot, t, par, ks, start, stop, rhs_hi=op_hi, rhs_lo=op_lo, ready=None):
                pe.wait_ge(hi_ready, c - 1)
                pe.wait_ge(lo_ready, c - 1)
                if start:
                    pe.wait_ge(acc_free, t - 1)
                for j, k in enumerate(ks):
                    if ready is not None:
                        ready(k)
                    last = products(par, slot, j, k, start and j == 0, stop and j == len(ks) - 1, rhs_hi, rhs_lo)
                last.then_inc(chunk_done, 1)

            pe.wait_ge(alr_w, 1)
            for k in range(KT):
                pe.wait_ge(op_rdy, k + 1)
                for n, x in enumerate((op_hi, op_lo)):
                    for a in range(2):
                        mm = nc.tensor.matmul(acc[0][:, a, 0:TH], alw[:, k, :], x[:, k, a * TH:(a + 1) * TH],
                                              start=(k == 0 and n == 0), stop=(k == KT - 1 and n == 1))
                        if k == KT - 1 and n == 1:
                            mm.then_inc(chunk_done, 1)
                if k % HK == 0:
                    pe.wait_ge(hi_ready, 1 + k // HK)
                    pe.wait_ge(lo_ready, 1 + k // HK)
                mm = products(1, 2 + k // HK, k % HK, k, k == 0, k == KT - 1, op_hi, op_lo)
                if k % HK == HK - 1:
                    mm.then_inc(chunk_done, 1)

            def ones_product(out2, buf):
                for a in range(2):
                    last = nc.tensor.matmul(out2[:, a, 0:TH], onesf[:], buf[:, a * TH:(a + 1) * TH],
                                            start=True, stop=True)
                return last

            def kd_transposes(i):
                w = P if i < 4 else TS
                for h in range(HEADS):
                    last = nc.tensor.transpose(g[1][0:w, h * P:(h + 1) * P], ex_g[:, h * w:(h + 1) * w], idn[:])
                return last

            def piece(kind, i):
                n = number((kind, i))
                before = order[:n - 1]
                if any(p[0] in V_KINDS for p in before):
                    pe.wait_ge(post_v, sum(p[0] in V_KINDS for p in before))
                if any(p[0] in A_KINDS for p in before):
                    pe.wait_ge(post_a, sum(p[0] in A_KINDS for p in before))
                if kind == "var1":
                    pe.wait_ge(zeroed, 6)
                    pe.wait_ge(sq_add, KT)
                    last = ones_product(g01, rstd[:])
                elif kind == "z":
                    pe.wait_ge(mid_in, 16 * 10)
                    pe.wait_ge(acc_free, 1)
                    for j in (range(4) if i == 0 else (4,)):
                        rows = P if j < 4 else TS
                        last = nc.tensor.matmul(g[j % 4][0:rows, :], alr[:, j * P:j * P + rows], wa2s,
                                                start=True, stop=True)
                elif kind == "b":
                    if i == 0:
                        pe.wait_ge(acc_free, T_CV)
                    if i >= 1:
                        kd_transposes(i - 1)
                    w, tr = (P, triu[:, 0:P]) if i < 4 else (TS, triu[0:TS, P:P + TS])
                    for h in range(HEADS):
                        last = nc.tensor.matmul(g[0][:, h * w:(h + 1) * w], loga[0:w, i, h * P:(h + 1) * P], tr,
                                                start=True, stop=True)
                elif kind == "kdt":
                    last = kd_transposes(4)
                elif kind == "mu":
                    pe.wait_ge(gelu_done, 4)
                    for a in range(2):
                        for h in range(4):
                            last = nc.tensor.matmul(g23[:, a, 0:TH], onesf[:], mix[:, 12 + h, a * TH:(a + 1) * TH],
                                                    start=(h == 0), stop=(h == 3))
                elif kind == "var_cm":
                    last = ones_product(g23, lnb)
                elif kind == "vvt":
                    for j in range(4):
                        for h in range(4):
                            last = nc.tensor.transpose(g[j][:, h * P:(h + 1) * P],
                                                       mix[:, 12 + h, j * P:(j + 1) * P], idn[:])
                elif kind == "zc":
                    if i == 0:
                        pe.wait_ge(zeroed, 8)
                        for h in range(4):
                            nc.tensor.transpose(g[0][0:TS, h * P:(h + 1) * P], mix[:, 12 + h, TP:T], idn[:])
                    for h in (range(3) if i == 0 else (3,)):
                        for j in range(4):
                            last = nc.tensor.matmul(g[(h + 1) % 4][:, j * P:(j + 1) * P], vvt[:, j, h * P:(h + 1) * P],
                                                    wmm[:, h * P:(h + 1) * P], start=True, stop=True)
                    if i == 1:
                        for h in range(4):
                            last = nc.tensor.matmul(g[1][:, h * TS:(h + 1) * TS], vvts[:, h * P:(h + 1) * P],
                                                    wsb[:, h, :], start=True, stop=True)
                elif kind == "vt":
                    pe.wait_ge(acc_free, T_V + i + 1)
                    for j in range(4):
                        nc.tensor.transpose(g[2][:, j * P:(j + 1) * P], tmp[:, i % 2, j * P:(j + 1) * P], idn[:])
                    last = nc.tensor.transpose(g[3][0:TS, 0:P], tmp[:, i % 2, TP:T], idn[:])
                elif kind == "p":
                    if i < NCHUNK:
                        r = CHUNK * (i % 2)
                        for h in range(HEADS):
                            last = nc.tensor.matmul(g[0][r:r + CHUNK, h * CHUNK:(h + 1) * CHUNK],
                                                    kT[:, h, CHUNK * i:CHUNK * (i + 1)],
                                                    qT[:, h, CHUNK * i:CHUNK * (i + 1)], start=True, stop=True)
                    if i >= 1:
                        m = i - 1
                        r, j = CHUNK * (m % 2), m // 2
                        for h in range(HEADS):
                            for e in range(2):
                                out = g[1][:, (2 * h + e) * CHUNK:(2 * h + e + 1) * CHUNK]
                                ve = v[r:r + CHUNK, j, h * DV + e * P:h * DV + (e + 1) * P]
                                nc.tensor.matmul(out, ve, AT[r:r + CHUNK, h * CHUNK:(h + 1) * CHUNK],
                                                 start=True, stop=(m == 0))
                                if m > 0:
                                    nc.tensor.matmul(out, S[:, h, e * P:(e + 1) * P],
                                                     qT[:, h, CHUNK * m:CHUNK * (m + 1)], start=False, stop=True)
                        for h in range(HEADS):
                            last = nc.tensor.matmul(g[2 + h // 2][:, (h % 2) * DV:(h % 2 + 1) * DV],
                                                    kd[r:r + CHUNK, j, h * P:(h + 1) * P],
                                                    v[r:r + CHUNK, j, h * DV:(h + 1) * DV], start=True, stop=True)
                elif kind == "s":
                    for h in range(HEADS) if i < 2 else ():
                        if i == 0:
                            last = nc.tensor.matmul(g[0][0:TS, h * TS:(h + 1) * TS], kT[:, h, TP:T], qT[:, h, TP:T],
                                                    start=True, stop=True)
                        else:
                            for e in range(2):
                                last = nc.tensor.matmul(g[0][:, (2 * h + e) * TS:(2 * h + e + 1) * TS],
                                                        vs[0:TS, h * DV + e * P:h * DV + (e + 1) * P],
                                                        ATs[:, h * TS:(h + 1) * TS], start=True, stop=True)
                    if i >= 2:
                        n = i - 2
                        h, half = n // 2, n % 2
                        pe.wait_ge(s0_in[n % 2], 16 * (n // 2 + 1))
                        for e in range(2):
                            for b in range(4):
                                col = TP + DS * (4 * half + b)
                                nc.tensor.matmul(g[0][:, e * 16 + b * DS:e * 16 + (b + 1) * DS],
                                                 S0[:, n % 2, b * DV + e * P:b * DV + (e + 1) * P],
                                                 qT[:, h, col:col + DS], start=True, stop=True)
                        for b in range(4):
                            last = nc.tensor.matmul(g[2 + b // 2][:, (b % 2) * DV:(b % 2 + 1) * DV], kdm[:, b, :],
                                                    vs[0:TS, h * DV:(h + 1) * DV], start=True, stop=True)
                elif kind == "on":
                    pe.wait_ge(osq_rdy, i + 1)
                    last = ones_product(g01, osq[:, 0, :])
                last.then_inc(inter, 1)

            for c in range(3, C_OUT):
                if c > 3:
                    t, half = c // 2, c % 2
                    chunk(c, c, t, t, range(HK * half, HK * (half + 1)), half == 0, half == 1)
                for kind, i in plan.get(c, ()):
                    piece(kind, i)

            def op_ready(base):
                def ready(k):
                    if k % 2 == 0:
                        pe.wait_ge(op_rdy, base + k + 2)
                return ready

            with pe.Fori(0, KT // 2) as i:
                for s in range(4):
                    half = s % 2
                    chunk(i * 4 + (C_OUT + s), C_OUT + s, i * 2 + (N_IN + s // 2), N_IN + s // 2,
                          range(HK * half, HK * (half + 1)), half == 0, half == 1,
                          ready=op_ready(KT) if s < 2 else None)

            def sum_squares(n_add):
                pe.wait_ge(hsq_add, n_add)
                ones_product(g01, rstd[:]).then_inc(var_done, 1)

            sum_squares(2 + KT)

            with pe.Fori(0, GROUPS) as gr:
                with pe.Fori(0, FG) as f:
                    for s in range(4):
                        half = s % 2
                        chunk(gr * C_GRP + f * 4 + (C_FF + s), C_FF + s,
                              gr * (C_GRP // 2) + f * 2 + (C_FF // 2 + s // 2), C_FF // 2 + s // 2,
                              range(HK * half, HK * (half + 1)), half == 0, half == 1,
                              ready=op_ready(2 * KT) if s < 2 else None)

                def hid_ready(k):
                    if k == 0:
                        pe.wait_ge(hid_rdy, gr * FG + (FG - 1))
                    if k == FG - 1:
                        pe.wait_ge(hid_rdy, gr * FG + FG)

                with pe.Fori(0, KT // 2) as i:
                    for s in range(4):
                        half = s % 2
                        chunk(gr * C_GRP + i * 4 + (C_FF + C_GU + s), C_FF + s,
                              gr * (C_GRP // 2) + i * 2 + ((C_FF + C_GU) // 2 + s // 2), (C_FF + C_GU) // 2 + s // 2,
                              range(DA * half, DA if half == 0 else FG), half == 0, half == 1,
                              hid_hi, hid_lo, ready=hid_ready)
            sum_squares(20 + KT)

        @block.vector
        def _(dve):
            own, took, freed = Count(), Count(), Count()

            def chain(ins):
                ins.then_inc(v_own, 1)
                dve.wait_ge(v_own, own.up())

            def take():
                dve.wait_ge(a_to_v, took.up())

            def f32(ap):
                return ap.bitcast(F32)

            def split_lo(c, slot):
                dve.wait_ge(hi_ready, c - 1)
                nc.vector.tensor_tensor(w_lo[:, slot % RING, :], w_raw[:, slot % RAW, :],
                                        f32(w_hi[:, slot % RING, :]), ALU.subtract).then_inc(lo_ready, 1)

            def op_lo_scaled(k, n, gcol):
                dve.wait_ge(op_h, n)
                nc.vector.scalar_tensor_tensor(out=op_lo[:, k, :], in0=trunk[:, k, :], scalar=vec[:, gcol:gcol + 1],
                                               in1=f32(op_hi[:, k, :]), op0=ALU.mult, op1=ALU.subtract)\
                    .then_inc(op_rdy, 1)

            dve.wait_ge(alr_hi, 1)
            nc.vector.tensor_tensor(alw[:, :, RANK:2 * RANK], al_raw.rearrange("p (k m) -> p k m", k=KT),
                                    f32(alw[:, :, 0:RANK]), ALU.subtract).then_inc(alr_w, 1)
            for k in range(KT):
                op_lo_scaled(k, k + 1, V_G1 + k)
                dve.wait_ge(sq_done, k + 1)
                if k == 0:
                    nc.vector.tensor_copy(rstd[:], tmp[:, 0, :]).then_inc(sq_add, 1)
                else:
                    dve.wait_ge(sq_add, k)
                    nc.vector.tensor_tensor(rstd[:], rstd[:], tmp[:, k % 2, :], ALU.add).then_inc(sq_add, 1)
                if k in (1, 3, 8, 12):
                    c = {1: 2, 3: 3, 8: 4, 12: 5}[k]
                    split_lo(c, c)

            def normalised(out, t, rows=P):
                nc.vector.tensor_tensor(out, acc[t % 2][0:rows, :, 0:TH], two(rstd[0:rows, :]), ALU.mult)\
                    .then_inc(acc_free, 1)

            def kd_out(i):
                if i < 4:
                    return nc.vector.tensor_copy(kd[:, i, :], g[1])
                return nc.vector.tensor_copy(vs[32:64, 0:HEADS * P], g[1][0:TS, :])

            def mask_kd(n):
                h, half = n // 2, n % 2
                return nc.vector.tensor_tensor(kdm[:], vs[32:64, h * P:(h + 1) * P].unsqueeze(1).to_broadcast([32, 4, P]),
                                               bm[32:64, 4 * half:4 * half + 4].unsqueeze(2).to_broadcast([32, 4, P]),
                                               ALU.mult)

            def out_square_sum(h):
                dve.wait_ge(osq_a, 2 * h + 2)
                nc.vector.tensor_tensor(osq[:, 0, :], osq[:, 0, :], osq[:, 1, :], ALU.add).then_inc(osq_rdy, 1)

            def post(kind, i):
                dve.wait_ge(inter, number((kind, i)))
                if kind == "var1":
                    dve.wait_ge(post_a, parts(A_KINDS, (kind, i)))
                    last = nc.vector.reciprocal(rstd[:], rstd[:])
                elif kind == "z":
                    for j in (range(4) if i == 0 else (4,)):
                        rows = P if j < 4 else TS
                        if j < 3:
                            take()
                        else:
                            dve.wait_ge(post_a, parts(A_KINDS, (kind, i)))
                        last = nc.vector.scalar_tensor_tensor(out=loga[0:rows, j, :], in0=g[j % 4][0:rows, :],
                                                              scalar=0.0, in1=loga[0:rows, j, :],
                                                              op0=ALU.min, op1=ALU.subtract)
                elif kind == "b":
                    w = P if i < 4 else TS
                    n, lc = (2, CHUNK) if i < 4 else (DB, DS)
                    tok = slice(i * P, i * P + w)
                    if i >= 1:
                        kd_out(i - 1)
                    take()
                    take()
                    chain(nc.vector.tensor_copy(ex_g[:, 0:4 * w], g[0][:, 0:4 * w]))
                    b4 = g[0][:, 0:4 * w].rearrange("p (a l) -> p a l", l=lc)
                    x4 = ex_g[:, 0:4 * w].rearrange("p (a l) -> p a l", l=lc)
                    nc.vector.tensor_tensor(x4, b4[:, :, lc - 1:lc].to_broadcast([P, HEADS * n, lc]), x4,
                                            ALU.subtract).then_inc(v_to_a, 1)
                    ends = ex_p[:, 0:4 * w].rearrange("p (h n l) -> p h n l", h=HEADS, n=n)[:, :, :, lc - 1]
                    dst = egp[:, 2 * i:2 * i + 2, :].rearrange("p n h -> p h n") if i < 4 else egs[:]
                    nc.vector.tensor_copy(dst, ends)

                    def heads(buf):
                        return buf[:, 0:4 * w].rearrange("p (h t) -> p h t", h=HEADS)

                    nc.vector.scalar_tensor_tensor(out=qT[:, :, tok], in0=qT[:, :, tok], scalar=DK ** -0.5,
                                                   in1=heads(ex_p), op0=ALU.mult, op1=ALU.mult)
                    dve.wait_ge(post_a, parts(A_KINDS, (kind, i)))
                    nc.vector.tensor_tensor(heads(ex_g), kT[:, :, tok], heads(ex_g), ALU.mult)
                    last = nc.vector.tensor_tensor(kT[:, :, tok], kT[:, :, tok], heads(ex_n), ALU.mult)
                elif kind == "kdt":
                    chain(kd_out(4))
                    last = mask_kd(0)
                elif kind == "mu":
                    dve.wait_ge(gelu_done, 4)
                    for h in range(4):
                        nc.vector.scalar_tensor_tensor(out=two(mix[:, 12 + h, :]), in0=g23[:, :, 0:TH],
                                                       scalar=-1.0 / (4 * P), in1=two(mix[:, 12 + h, :]),
                                                       op0=ALU.mult, op1=ALU.add).then_inc(v_to_a, 1)
                    for h in range(4):
                        if h < 3:
                            dve.wait_ge(cm_sq, h + 1)
                        else:
                            dve.wait_ge(post_a, parts(A_KINDS, (kind, i)))
                        if h == 0:
                            last = nc.vector.tensor_copy(lnb, tmp[:, 0, :])
                        else:
                            dve.wait_ge(cm_add, h)
                            last = nc.vector.tensor_tensor(lnb, lnb, tmp[:, h % 2, :], ALU.add)
                        if h < 3:
                            last.then_inc(cm_add, 1)
                elif kind == "var_cm":
                    dve.wait_ge(post_a, parts(A_KINDS, (kind, i)))
                    chain(nc.vector.reciprocal(lnb, lnb))
                    for h in range(4):
                        last = nc.vector.scalar_tensor_tensor(out=mix[:, 12 + h, :], in0=mix[:, 12 + h, :],
                                                              scalar=vec[:, V_LG + h:V_LG + h + 1], in1=lnb,
                                                              op0=ALU.mult, op1=ALU.mult)
                    chain(last)
                    for h in range(4):
                        last = nc.vector.tensor_scalar(mix[:, 12 + h, :], mix[:, 12 + h, :],
                                                       vec[:, V_LB + h:V_LB + h + 1], None, ALU.add)
                elif kind == "vvt":
                    nc.vector.tensor_copy(vvt[:, 0, :], g[0])
                    last = nc.vector.tensor_copy(vvt[:, 1, :], g[1])
                elif kind == "zc":
                    if i == 0:
                        nc.vector.tensor_copy(vvts[:], g[0][0:TS, :])
                    hs = range(3) if i == 0 else (3,)
                    for h in hs:
                        last = nc.vector.tensor_tensor(
                            mix[:, 12 + h, 0:TP].rearrange("p (j t) -> p j t", j=4),
                            g[(h + 1) % 4].rearrange("p (j t) -> p j t", j=4),
                            bsb[:, h * P:(h + 1) * P].unsqueeze(1).to_broadcast([P, 4, P]), ALU.add)
                    if i == 1:
                        dve.wait_ge(cmv_out, 16)
                        for h in range(4):
                            last = nc.vector.tensor_tensor(
                                mix[:, 12 + h, TP:T].rearrange("p (b t) -> p b t", b=DB),
                                g[1][:, h * TS:(h + 1) * TS].rearrange("p (b t) -> p b t", b=DB),
                                bsb[:, h * P:h * P + DS].unsqueeze(1).to_broadcast([P, DB, DS]), ALU.add)
                    if i == 1:
                        chain(last)
                        dve.wait_ge(gelu_done, 8)
                        for h in range(4):
                            last = nc.vector.tensor_tensor(mix[:, 12 + h, :], mix[:, 12 + h, :], mix[:, 8 + h, :],
                                                           ALU.mult)
                            last.then_inc(mix_done, 1)
                        dve.wait_ge(mix_done, 4)
                        last = None
                elif kind == "vt":
                    nc.vector.tensor_copy(v[:, 0:4, i * P:(i + 1) * P], g[2].rearrange("p (j e) -> p j e", j=4))
                    last = nc.vector.tensor_copy(vs[0:TS, i * P:(i + 1) * P], g[3][0:TS, 0:P])
                elif kind == "p":
                    if i < NCHUNK:
                        r = CHUNK * (i % 2)
                        last = nc.vector.copy_predicated(AT[r:r + CHUNK, :], mA[r:r + CHUNK, :],
                                                         g[0][r:r + CHUNK, 0:HEADS * CHUNK])
                    for h in range(HEADS) if i >= 1 else ():
                        ds = g[2 + h // 2][:, (h % 2) * DV:(h % 2 + 1) * DV]
                        if i == 1:
                            last = nc.vector.tensor_copy(S[:, h, :], ds)
                        else:
                            last = nc.vector.scalar_tensor_tensor(out=S[:, h, :], in0=S[:, h, :],
                                                                  scalar=egp[:, i - 1, h:h + 1], in1=ds,
                                                                  op0=ALU.mult, op1=ALU.add)
                elif kind == "s":
                    if i == 0:
                        last = nc.vector.copy_predicated(ATs[:], mS[:], g[0][0:TS, 0:HEADS * TS])
                    elif i == 1:
                        last = None
                    else:
                        n = i - 2
                        h, half = n // 2, n % 2
                        o = mix[:, 2 * h:2 * h + 2, TP + 16 * half:TP + 16 * (half + 1)]
                        nc.vector.tensor_tensor(o, g[0][:, 0:32].rearrange("p (e t) -> p e t", e=2), o, ALU.add)
                        if n + 1 < 8:
                            mask_kd(n + 1)
                        for b in range(4):
                            last = nc.vector.scalar_tensor_tensor(
                                out=S0[:, n % 2, b * DV:(b + 1) * DV], in0=S0[:, n % 2, b * DV:(b + 1) * DV],
                                scalar=egs[:, h, 4 * half + b:4 * half + b + 1],
                                in1=g[2 + b // 2][:, (b % 2) * DV:(b % 2 + 1) * DV], op0=ALU.mult, op1=ALU.add)
                elif kind == "on":
                    dve.wait_ge(post_a, parts(A_KINDS, (kind, i)))
                    chain(nc.vector.reciprocal(orstd, orstd))
                    if i < 3:
                        out_square_sum(i + 1)
                    for e in range(2):
                        m = 2 * i + e
                        last = nc.vector.scalar_tensor_tensor(out=mix[:, m, :], in0=mix[:, m, :],
                                                              scalar=vec[:, V_GLA + m:V_GLA + m + 1], in1=orstd,
                                                              op0=ALU.mult, op1=ALU.mult)
                if last is None:
                    last = dve.nop()
                last.then_inc(post_v, 1)

            zpp = zp[:, 0:2 + TP]
            zps = zp[:, 2 + TP:].rearrange("p (b t) -> p b t", b=DB)

            def conv_tile(i):
                nc.vector.tensor_tensor(zpp[:, 2:], tmp[:, 0, 0:TP], tmp[:, 1, 0:TP], ALU.mult)
                nc.vector.tensor_tensor(zps[:, :, 2:], tmp[:, 0, TP:T].rearrange("p (b t) -> p b t", b=DB),
                                        tmp[:, 1, TP:T].rearrange("p (b t) -> p b t", b=DB), ALU.mult)
                chain(nc.vector.tensor_copy(zps[:, :, 0:2], cbs[:, i, :].rearrange("p (b t) -> p b t", b=DB)))
                mp = mix[:, 8 + i, 0:TP]
                ms = mix[:, 8 + i, TP:T].rearrange("p (b t) -> p b t", b=DB)
                for z, m, n in ((zpp, mp, TP), (zps, ms, DS)):
                    def tap(j):
                        return z[:, j:j + n] if n == TP else z[:, :, j:j + n]
                    for j in range(3):
                        w = vec[:, V_CW + 4 * j + i:V_CW + 4 * j + i + 1]
                        if j == 0:
                            chain(nc.vector.tensor_scalar(m, tap(0), w, vec[:, V_CB + i:V_CB + i + 1],
                                                          ALU.mult, ALU.add))
                        else:
                            chain(nc.vector.scalar_tensor_tensor(out=m, in0=tap(j), scalar=w, in1=m,
                                                                 op0=ALU.mult, op1=ALU.add))
                nc.vector.tensor_copy(cst[:, i, 0:2], zpp[:, TP:TP + 2])
                nc.vector.tensor_copy(cst[:, i, 2:].rearrange("p (b t) -> p b t", b=DB), zps[:, :, DS:DS + 2])

            def evac(t):
                if t == 0:
                    normalised(two(alr[0:2 * RANK, :]), 0, 2 * RANK)
                elif t < T_CV:
                    normalised(two((qT if t < T_K else kT)[:, (t - T_Q) % 4, :]), t)
                elif t < T_V:
                    j = t - T_CV
                    m = mix[:, 12 + j if t < T_CU else 4 + j, :]
                    normalised(two(m), t)
                    dve.wait_ge(acc_free, t + 1)
                    dve.nop().then_inc(v_to_a, 1)
                elif t < T_CONV:
                    normalised(two(tmp[:, (t - T_V) % 2, :]), t)
                elif t < T_R:
                    i, part = divmod(t - T_CONV, 3)
                    normalised(two(tmp[:, 1 if part == 1 else 0, :]), t)
                    if part >= 1:
                        dve.wait_ge(acc_free, t + 1)
                    if part == 1:
                        conv_tile(i)
                    if part == 2:
                        nc.vector.tensor_tensor(mix[:, 8 + i, :], mix[:, 8 + i, :], tmp[:, 0, :], ALU.mult)\
                            .then_inc(mix_done, 1)
                else:
                    i = t - T_R
                    normalised(two(tmp[:, i % 2, :]), t)
                    dve.wait_ge(acc_free, t + 1)
                    dve.nop().then_inc(v_to_a, 1)
                    dve.wait_ge(silu_r, i + 1)
                    nc.vector.tensor_tensor(mix[:, i, :], mix[:, i, :], tmp[:, i % 2, :], ALU.mult)\
                        .then_inc(mix_done, 1)

            def op_lo_tile(k):
                dve.wait_ge(op_h, KT + k + 1)
                nc.vector.tensor_tensor(op_lo[:, k, :], mix[:, osl(k), :], f32(op_hi[:, k, :]), ALU.subtract)\
                    .then_inc(op_rdy, 1)

            for c in range(2, C_OUT):
                dve.wait_ge(chunk_done, c + 1)
                if c == C_OUT - 1:
                    split_lo(c + 4, c + 4)
                    for k in range(8):
                        op_lo_tile(k)
                    evac(c // 2)
                    for k in range(8, KT):
                        op_lo_tile(k)
                    continue
                if c % 2 and c > 3:
                    evac(c // 2)
                for kind, i in plan.get(c, ()):
                    if kind in V_KINDS:
                        post(kind, i)
                if c == 3:
                    dve.wait_ge(post_v, parts(V_KINDS, ("var1", 0)))
                    evac(0)
                    evac(1)
                if c == OSQ_AT:
                    out_square_sum(0)
                split_lo(c + 4, c + 4)

            def zero_sum(n_read):
                dve.wait_ge(acc_free, n_read)
                nc.vector.memset(rstd[:], 0.0).then_inc(hsq_add, 2)

            def residual(t, par, m, squares=None):
                dve.wait_ge(acc_free, t)
                nc.vector.tensor_tensor(two(trunk[:, m, :]), acc[par % 2][:, :, 0:TH], two(trunk[:, m, :]), ALU.add)\
                    .then_inc(acc_free, 1)
                if squares is not None:
                    h_base, add_base = squares
                    dve.wait_ge(acc_free, t + 1)
                    dve.nop().then_inc(h_done, 1)
                    dve.wait_ge(hsq_done, m + (h_base + 1))
                    dve.wait_ge(hsq_add, m + add_base)
                    nc.vector.tensor_tensor(rstd[:], rstd[:], tmp[:, par_of(m, par), :], ALU.add)\
                        .then_inc(hsq_add, 1)

            def par_of(m, par):
                return (par + 1) % 2

            def reciprocal_std(n):
                dve.wait_ge(std_done, n)
                nc.vector.reciprocal(rstd[:], rstd[:]).then_inc(rstd_ok, 1)

            zero_sum(N_IN)
            dve.wait_ge(x_back, 16 * 4)
            with dve.Fori(0, KT // 2) as i:
                for s in range(4):
                    c = i * 4 + (C_OUT + s)
                    dve.wait_ge(chunk_done, c + 1)
                    if s % 2:
                        residual(i * 2 + (N_IN + s // 2), N_IN + s // 2, i * 2 + s // 2, (0, 2))
                    split_lo(c + 4, C_OUT + s + 4)
            for k in range(KT):
                op_lo_scaled(k, 2 * KT + k + 1, V_G2 + k)
            reciprocal_std(1)

            def group(gr, last):
                with dve.Fori(0, FG) as f:
                    for s in range(4):
                        c = gr * C_GRP + f * 4 + (C_FF + s)
                        t = gr * (C_GRP // 2) + f * 2 + (C_FF // 2 + s // 2)
                        par = C_FF // 2 + s // 2
                        dve.wait_ge(chunk_done, c + 1)
                        if s == 1:
                            dve.wait_ge(rstd_ok, 1)
                            normalised(two(tmp[:, 1, :]), par)
                        if s == 3:
                            normalised(two(tmp[:, 0, :]), par)
                            dve.wait_ge(acc_free, t + 1)
                            dve.wait_ge(gate_act, gr * FG + f + 1)
                            nc.vector.tensor_tensor(tmp[:, 0, :], tmp[:, 0, :], tmp[:, 1, :], ALU.mult)\
                                .then_inc(hid_f, 1)
                            dve.wait_ge(hid_h, gr * FG + f + 1)
                            nc.vector.tensor_tensor(hid_lo[:, f, :], tmp[:, 0, :], f32(hid_hi[:, f, :]),
                                                    ALU.subtract).then_inc(hid_rdy, 1)
                        split_lo(c + 4, C_FF + s + 4)

                def down(i, tail):
                    for s in range(4):
                        c = gr * C_GRP + i * 4 + (C_FF + C_GU + s)
                        dve.wait_ge(chunk_done, c + 1)
                        if s % 2:
                            t0 = (C_FF + C_GU) // 2 + s // 2
                            residual(gr * (C_GRP // 2) + i * 2 + t0, t0, i * 2 + s // 2, (KT, 20) if last else None)
                        if not tail:
                            split_lo(c + 4, C_FF + s + 4)

                if last:
                    zero_sum(gr * (C_GRP // 2) + (C_FF + C_GU) // 2)
                with dve.Fori(0, KT // 2 - (1 if last else 0)) as i:
                    down(i, False)
                if last:
                    down(KT // 2 - 1, True)

            with dve.Fori(0, GROUPS - 1) as gr:
                group(gr, False)
            group(GROUPS - 1, True)
            reciprocal_std(2)
            dve.wait_ge(rstd_ok, 2)
            for k in range(KT):
                nc.vector.scalar_tensor_tensor(out=trunk[:, k, :], in0=trunk[:, k, :],
                                               scalar=vec[:, V_GF + k:V_GF + k + 1], in1=rstd[:],
                                               op0=ALU.mult, op1=ALU.mult).then_inc(out_rdy, 1)


INS = ("xT", "w_alr", "w_in", "w_out", "w_gu", "w_da", "w_db", "vecs", "wa2", "wm", "wsbd", "bs", "s0", "cbuf",
       "ident", "tri", "maskA", "maskS", "bmask")
OUTS = (("yT", (P, KT, T)), ("gla_p", (HEADS, DK, DV)), ("gla_s", (HEADS, 2, P, 4 * DV)),
        ("conv_o", (P, 4, 2 + 2 * DB)), ("cmv", (P, 4, TS)))


def kernel(**inputs):
    import numpy as np
    import concourse.bacc as bacc
    from concourse.bass_utils import run_bass_kernel_spmd

    a = {k: np.asarray(x) for k, x in inputs.items()}

    def feature_major(x):
        return x.reshape(x.shape[0], -1, P).transpose(2, 1, 0)

    def tiles(w):
        k, m = w.shape
        return w.reshape(2, k // P // 2, P, m // P, P).transpose(3, 0, 2, 1, 4).reshape(m // P * 2, P, -1)

    x = np.concatenate([a["x_prompt"].reshape(TP, D), a["x_sample"].reshape(TS, D)])
    w = a["w_in"][0]
    parts, at = [], 0
    for n in (HEADS * DK, HEADS * DK, HEADS * DV, HEADS * DV, RANK, 512, 512, 512, 512, 512):
        parts.append(w[:, at:at + n])
        at += n
    wq, wk, wv, wr, wal, wcb, wcc, wch, wcu, wcv = parts
    conv = np.concatenate([y[:, i * P:(i + 1) * P] for i in range(4) for y in (wcc, wch, wcb)], axis=1)
    win = tiles(np.concatenate([wq, wk, wcv, wcu, wv, conv, wr], axis=1))
    wo = a["w_out"][0].reshape(KT, P, D)[MIX_ORDER].reshape(D, D)
    gu = np.stack([a["w_gate"][0].reshape(D, FT, P), a["w_up"][0].reshape(D, FT, P)], axis=2).reshape(D, 2 * DFF)
    wd = a["w_down"][0].reshape(GROUPS, FG, P, KT, P).transpose(0, 3, 2, 1, 4)
    cols = [feature_major(a[n].reshape(-1, size))[:, :, j] for n, size in
            (("norm1_g", D), ("norm2_g", D), ("final_g", D), ("gla_g", HEADS * DV), ("conv_w", 512), ("conv_b", 512),
             ("cm_ln_g", 512), ("cm_ln_b", 512)) for j in range(a[n].size // size)]
    ws = a["cm_ws"][0]
    wsbd = np.zeros((TS, 4, TS), ws.dtype)
    for b in range(DB):
        wsbd[b * DS:(b + 1) * DS, :, b * DS:(b + 1) * DS] = ws[:, :DS, :DS].transpose(2, 0, 1)
    s, t = np.arange(P)[:, None], np.arange(P)[None, :]
    tri = ((s <= t) & (s // CHUNK == t // CHUNK)) / 16.0
    tri_s = ((s <= t) & (s // DS == t // DS))[:, :TS] / 16.0
    arrays = {
        "xT": feature_major(x),
        "w_alr": wal.reshape(KT, P, RANK).transpose(1, 0, 2),
        "w_in": win,
        "w_out": tiles(wo),
        "w_gu": tiles(gu),
        "w_da": wd[:, :, :, :DA].reshape(GROUPS * KT, P, DA * P),
        "w_db": wd[:, :, :, DA:].reshape(GROUPS * KT, P, (FG - DA) * P),
        "vecs": np.concatenate(cols, axis=1),
        "wa2": np.concatenate([a["w_a2"][0], a["w_a2"][0], a["b_a"][:1]]),
        "wm": ws.transpose(2, 0, 1).reshape(P, 4 * P),
        "wsbd": wsbd,
        "bs": a["cm_bs"][0].reshape(4 * P),
        "s0": a["state_gla"][0].reshape(2, 4, HEADS, DK, DV).transpose(2, 0, 3, 1, 4).reshape(HEADS, 2, P, 4 * DV),
        "cbuf": a["state_conv"][0].reshape(2 * DB, 4, P).transpose(2, 1, 0),
        "ident": np.eye(P, dtype=np.float32),
        "tri": np.concatenate([tri, tri_s], axis=1).astype(np.float32),
        "maskA": np.tile(s % CHUNK <= t[:, :CHUNK], (1, HEADS)).astype(np.int32),
        "maskS": np.tile(((s <= t) & (s // DS == t // DS))[:TS, :TS], (1, HEADS)).astype(np.int32),
        "bmask": (s[:TS] // DS == t[:, :DB]).astype(np.float32),
    }
    arrays = {n: np.ascontiguousarray(y) for n, y in arrays.items()}
    nc = bacc.Bacc("TRN2", target_bir_lowering=False, num_devices=1, dynamic_dma_scratch_size=1024)
    args = [nc.dram_tensor(n, arrays[n].shape, mybir.dt.from_np(arrays[n].dtype), kind="ExternalInput").ap()
            for n in INS]
    args += [nc.dram_tensor(n, shape, F32, kind="ExternalOutput").ap() for n, shape in OUTS]
    build(nc, *args)
    r = run_bass_kernel_spmd(nc, [arrays], core_ids=[0]).results[0]
    y = r["yT"].transpose(2, 1, 0).reshape(T, D)
    cst = r["conv_o"].transpose(2, 1, 0).reshape(2 + 2 * DB, 512)
    gs = r["gla_s"].reshape(HEADS, 2, DK, 4, DV).transpose(1, 3, 0, 2, 4).reshape(1, DB, HEADS, DK, DV)
    return (y[:TP].reshape(1, TP, D), y[TP:].reshape(DB, DS, D), r["gla_p"].reshape(1, 1, HEADS, DK, DV),
            cst[:2].reshape(1, 1, 2, 512), gs, cst[2:].reshape(1, DB, 2, 512),
            r["cmv"].transpose(2, 1, 0).reshape(1, DB, DS, 512))
```

```python
from contextlib import ExitStack

import concourse.bass as bass
from concourse import mybir

F32 = mybir.dt.float32
F32R = mybir.dt.float32r
I32 = mybir.dt.int32
ALU = mybir.AluOpType
ACT = mybir.ActivationFunctionType

P = 128
D = 2048
KT = D // P
TP = 512
DB, DS = 8, 4
TS = DB * DS
T = TP + TS
TH = T // 2
HEADS, DK, DV, RANK = 4, 128, 256, 16
CHUNK = 64
NCHUNK = TP // CHUNK
PAIRS = NCHUNK // 2
CMC = 128
DFF = 5632
FT = DFF // P
GROUPS = 4
FG = FT // GROUPS
EPS = 1e-6

T_Q, T_K, T_CV, T_CU, T_V, T_CONV, T_R, N_IN = 1, 5, 9, 13, 17, 25, 37, 45
HK = KT // 2
CH = HK * P
RING = 4
RAW = 2
C_OUT = 2 * N_IN
C_FF = C_OUT + 2 * KT
C_GU = 4 * FG
C_GRP = C_GU + 2 * KT
C_END = C_FF + GROUPS * C_GRP
DA = (FG + 1) // 2
MIX_ORDER = list(range(HK, KT)) + list(range(HK))

VAR1_AT = 6
Z_AT = (8, 11)
B_AT = (19, 21, 23, 25, 27)
KDT_AT = 29
MU_AT, VAR_CM_AT, VVT_AT, ZC_AT = 28, 31, 34, (36, 38)
VT_AT = tuple(37 + 2 * i for i in range(8))
P_AT = (53, 57, 61, 65)
S_AT = tuple(50 + 2 * i for i in range(10))
OSQ_AT = 69
ON_AT = (71, 73, 75, 77)

NV_OUT = 12
SPLIT_AT = {1: 2, 3: 3, 10: 4, 15: 5}

V_G1, V_G2, V_GF, V_GLA, V_CW, V_CB, V_LG, V_LB, NV = 0, 16, 32, 48, 56, 68, 72, 76, 80


A_KINDS = ("var1", "z", "b", "mu", "var_cm", "vvt", "p", "s", "on")
V_KINDS = A_KINDS + ("kdt", "zc", "vt")


def mixer_plan():
    plan = {}
    for kind, places in (("var1", (VAR1_AT,)), ("z", Z_AT), ("b", B_AT), ("kdt", (KDT_AT,)), ("mu", (MU_AT,)),
                         ("var_cm", (VAR_CM_AT,)), ("vvt", (VVT_AT,)), ("zc", ZC_AT), ("vt", VT_AT), ("p", P_AT),
                         ("s", S_AT), ("on", ON_AT)):
        for i, c in enumerate(places):
            plan.setdefault(c, []).append((kind, i))
    order = [piece for c in sorted(plan) for piece in plan[c]]
    return plan, order


class Count:

    def __init__(self):
        self.n = 0

    def up(self):
        self.n += 1
        return self.n


def build(nc, xT, w_alr, w_in, w_out, w_gu, w_da, w_db, vecs, wa2, wm, wsbd, bs, s0, cbuf, ident, tri, maskA, maskS,
          bmask, yT, gla_p, gla_s, conv_o, cmv):
    with ExitStack() as ctx:
        def sb(name, shape, dt=F32):
            return ctx.enter_context(nc.sbuf_tensor(name, shape, dt))

        def sem(name):
            return ctx.enter_context(nc.semaphore(name))

        trunk = sb("trunk", [P, KT, T])
        op_hi = sb("op_hi", [P, KT, T], F32R)
        op_lo = sb("op_lo", [P, KT, T], F32R)
        w_raw = sb("w_raw", [P, RAW, CH])
        w_hi = sb("w_hi", [P, RING, CH], F32R)
        w_lo = sb("w_lo", [P, RING, CH], F32R)
        vec = sb("vec", [P, NV])
        idn = sb("idn", [P, P])
        onesf = sb("onesf", [P, P])
        rstd = sb("rstd", [P, T])
        tmp = sb("tmp", [P, 2, T])
        cst = sb("cst", [P, 4, 2 + 2 * DB])
        with ExitStack() as ff:
            hid_hi = ff.enter_context(nc.sbuf_tensor("hid_hi", [P, FG, T], F32R))
            hid_lo = ff.enter_context(nc.sbuf_tensor("hid_lo", [P, FG, T], F32R))
        mix = sb("mix", [P, KT, T])
        kd = sb("kd", [P, 4, HEADS * DK])
        vs = sb("vs", [TS, HEADS * DV])
        vs4 = sb("vs4", [P, HEADS * DV], F32R)
        kd4 = sb("kd4", [P, HEADS * DK], F32R)
        S = sb("S", [P, HEADS, DV])
        with nc.sbuf_tensor("alw", [P, KT, P], F32R) as alw:
            pass
        S0 = sb("S0", [P, 2, 4 * DV])
        kdm = sb("kdm", [P, 4, DK], F32R)
        ATs = sb("ATs", [32, HEADS * TS])
        triu = sb("triu", [P, P + TS])
        mA = sb("mA", [P, HEADS * CHUNK], I32)
        mS = sb("mS", [32, HEADS * TS], I32)
        bm = sb("bm", [P, DB])
        egp = sb("egp", [P, NCHUNK, HEADS])
        egs = sb("egs", [P, HEADS, DB])
        wsb = sb("wsb", [32, 4, TS])
        zp = sb("zp", [P, 2 + TP + DB * (2 + DS)])
        cbs = sb("cbs", [P, 4, 2 * DB])
        trf = trunk[:].rearrange("p k t -> p (k t)")
        qT = trf[:, 0:HEADS * T].rearrange("p (h t) -> p h t", h=HEADS)
        kT = trf[:, HEADS * T:2 * HEADS * T].rearrange("p (h t) -> p h t", h=HEADS)
        AT = kT
        v = trf[:, 2 * HEADS * T:2 * HEADS * T + 4 * HEADS * DV].rearrange("p (j e) -> p j e", j=4)
        mxf = mix[:].rearrange("p k t -> p (k t)")
        loga = mxf[:, 0:5 * 512].rearrange("p (j d) -> p j d", j=5)
        ex_g, ex_p, ex_n = (mxf[:, (5 + i) * 512:(6 + i) * 512] for i in range(3))
        vvts = mxf[0:TS, 5 * 512:6 * 512]
        vvt = S0[:].rearrange("p a (b c) -> p (a b) c", b=2)
        wmm = S[:].rearrange("p h e -> p (h e)")[:, 0:512]
        bsb = S[:].rearrange("p h e -> p (h e)")[:, 512:1024]
        kdf = kd[:].rearrange("p j d -> p (j d)")
        alr = kdf[0:2 * RANK + 1, 0:T]
        wa2s = kdf[0:2 * RANK + 1, T:T + HEADS * DK]
        lnb = zp[:, 2:2 + T]
        osq = kdf[:, 0:2 * T].rearrange("p (a t) -> p a t", a=2)
        orstd = kdf[:, 2 * T:3 * T]
        al_raw = tmp[:].rearrange("p a t -> p (a t)")[:, 0:KT * RANK]
        acc = [ctx.enter_context(nc.psum_tensor(f"acc{i}", [P, 2, 512], F32)) for i in range(2)]
        g01 = ctx.enter_context(nc.psum_tensor("g01", [P, 2, 512], F32))
        g23 = ctx.enter_context(nc.psum_tensor("g23", [P, 2, 512], F32))
        g = [g01[:, 0, :], g01[:, 1, :], g23[:, 0, :], g23[:, 1, :]]

        def accv(t):
            return acc[t % 2][:, :, 0:TH]

        def two(ap):
            return ap.rearrange("p (a t) -> p a t", a=2)

        consts_in = sem("consts_in")
        alr_w_in = sem("alr_w_in")
        mid_in = sem("mid_in")
        x_in = [sem(f"x_in{i}") for i in range(8)]
        w_landed = [sem(f"w_landed{i}") for i in range(RAW)]
        hi_ready = sem("hi_ready")
        lo_ready = sem("lo_ready")
        zeroed = sem("zeroed")
        alr_hi = sem("alr_hi")
        alr_w = sem("alr_w")
        op_h = sem("op_h")
        op_rdy = sem("op_rdy")
        sq_done = sem("sq_done")
        sq_add = sem("sq_add")
        chunk_done = sem("chunk_done")
        acc_free = sem("acc_free")
        inter = sem("inter")
        post_v = sem("post_v")
        post_a = sem("post_a")
        v_to_a = sem("v_to_a")
        a_to_v = sem("a_to_v")
        v_own = sem("v_own")
        a_own = sem("a_own")
        gelu_done = sem("gelu_done")
        cm_sq = sem("cm_sq")
        cm_add = sem("cm_add")
        cmv_out = sem("cmv_out")
        silu_r = sem("silu_r")
        osq_a = sem("osq_a")
        osq_rdy = sem("osq_rdy")
        mix_done = sem("mix_done")
        s0_in = [sem(f"s0_in{i}") for i in range(2)]
        s0_out = [sem(f"s0_out{i}") for i in range(2)]
        x_back = sem("x_back")
        h_done = sem("h_done")
        hsq_done = sem("hsq_done")
        hsq_add = sem("hsq_add")
        var_done = sem("var_done")
        std_done = sem("std_done")
        rstd_ok = sem("rstd_ok")
        gate_act = sem("gate_act")
        hid_f = sem("hid_f")
        hid_h = sem("hid_h")
        hid_rdy = sem("hid_rdy")
        y_scaled = sem("y_scaled")
        factor_half = sem("factor_half")
        factor_psum = sem("factor_psum")
        out_v = sem("out_v")
        out_p = sem("out_p")
        stored = sem("stored")

        plan, order = mixer_plan()

        def number(piece):
            return order.index(piece) + 1

        def parts(kinds, piece):
            return sum(p[0] in kinds for p in order[:number(piece)])

        def landed(c, slot):
            return c * 8 - 8 * (slot % RAW)

        def osl(k):
            return MIX_ORDER[k]

        block = ctx.enter_context(nc.Block())

        @block.sync
        def _(sp):
            def load(slot, src, c, cols=CH):
                if not isinstance(c, int) or c >= 4:
                    sp.wait_ge(hi_ready, c - 3)
                    sp.wait_ge(lo_ready, c - 3)
                sp.dma_start(w_raw[:, slot % RAW, 0:cols], src).then_inc(w_landed[slot % RAW], 16)

            def load_x(i):
                sp.dma_start(trunk[:, 2 * i:2 * i + 2, :], xT[:, 2 * i:2 * i + 2, :]).then_inc(x_in[i], 16)

            sp.dma_start(vec[:], vecs).then_inc(consts_in, 16)
            load_x(0)
            sp.dma_start(al_raw, w_alr.rearrange("p k m -> p (k m)")).then_inc(alr_w_in, 16)
            load(2, w_in[0], 2)
            load_x(1)
            load(3, w_in[1], 3)
            for i in range(2, 8):
                load_x(i)
                if i in (3, 5):
                    load(4 + i // 4, w_in[2 + i // 4], 4 + i // 4)
            for dst, src in ((idn[:], ident), (triu[:], tri), (mA[:], maskA), (mS[:], maskS), (bm[:], bmask),
                             (wa2s, wa2), (wmm, wm), (wsb[:], wsbd), (bsb, bs.partition_broadcast(P)),
                             (cbs[:], cbuf)):
                sp.dma_start(dst, src).then_inc(mid_in, 16)

            def s0_dram(t, i):
                return t[i // 2, i % 2]

            def store_s0(i):
                sp.wait_ge(post_v, parts(V_KINDS, ("s", i + 2)))
                sp.dma_start(s0_dram(gla_s, i), S0[:, i % 2, :]).then_inc(s0_out[i % 2], 16)

            def load_s0(i):
                if i >= 2:
                    sp.wait_ge(s0_out[i % 2], 16 * (i // 2))
                else:
                    sp.wait_ge(inter, number(("zc", 1)))
                sp.dma_start(S0[:, i % 2, :], s0_dram(s0, i)).then_inc(s0_in[i % 2], 16)

            for c in range(6, C_OUT):
                if c == ZC_AT[1] + 8:
                    load_s0(0)
                    load_s0(1)
                for i in range(8):
                    if c == S_AT[2 + i] + 7:
                        store_s0(i)
                    if c == S_AT[2 + i] + 8 and i + 2 < 8:
                        load_s0(i + 2)
                if c == S_AT[-1] + 8:
                    sp.wait_ge(post_v, parts(V_KINDS, ("p", PAIRS - 1)))
                    sp.dma_start(gla_p.rearrange("h d e -> d h e"), S[:]).then_inc(stored, 16)
                    sp.wait_ge(inter, number(("s", 9)))
                    for i in range(4):
                        sp.dma_start(trunk[:, 4 * i:4 * i + 4, :], xT[:, 4 * i:4 * i + 4, :]).then_inc(x_back, 16)
                load(c, w_in[c - 2], c)
            with sp.Fori(0, KT // 2) as i:
                for s in range(4):
                    load(C_OUT + s, w_out[i * 4 + s], i * 4 + (C_OUT + s))
            sp.wait_ge(mix_done, 8)
            sp.dma_start(conv_o, cst[:]).then_inc(stored, 16)
            with sp.Fori(0, GROUPS) as gr:
                with sp.Fori(0, FG) as f:
                    for s in range(4):
                        load(C_FF + s, w_gu[gr * C_GU + f * 4 + s], gr * C_GRP + f * 4 + (C_FF + s))
                with sp.Fori(0, KT // 2) as i:
                    for s in range(4):
                        m = gr * KT + i * 2 + s // 2
                        src, cols = (w_db[m], (FG - DA) * P) if s % 2 else (w_da[m], DA * P)
                        load(C_FF + s, src, gr * C_GRP + i * 4 + (C_FF + C_GU + s), cols)
            for i in [j for pair in zip(range(NV_OUT // 2), list(range(NV_OUT // 2, 8)) + [None] * 8) for j in pair
                      if j is not None]:
                if 2 * i < NV_OUT:
                    sp.wait_ge(out_v, 2 * i + 2)
                else:
                    sp.wait_ge(out_p, 2 * i + 2 - NV_OUT)
                sp.dma_start(yT[:, 2 * i:2 * i + 2, :], trunk[:, 2 * i:2 * i + 2, :]).then_inc(stored, 16)
            sp.wait_ge(stored, 16 * (1 + 1 + 8))
            sp.wait_ge(cmv_out, 16)
            sp.wait_ge(s0_out[0], 16 * 4)
            sp.wait_ge(s0_out[1], 16 * 4)

        @block.gpsimd
        def _(pool):
            nc.gpsimd.memset(cst[0:1, 0, 0:1], 0.0).then_inc(zeroed, 1)
            pool.wait_ge(zeroed, 1)
            nc.gpsimd.memset(alw[:].bitcast(F32), 0.0).then_inc(zeroed, 1)
            nc.gpsimd.memset(onesf[:], 1.0).then_inc(zeroed, 1)
            nc.gpsimd.memset(ATs[:], 0.0).then_inc(zeroed, 1)
            pool.wait_ge(zeroed, 4)
            nc.gpsimd.memset(alr[2 * RANK:2 * RANK + 1, :], 1.0).then_inc(zeroed, 1)
            pool.wait_ge(zeroed, 5)
            nc.gpsimd.memset(zp[:, 0:2], 0.0).then_inc(zeroed, 1)
            pool.wait_ge(zeroed, 6)
            pool.wait_ge(mid_in, 16 * 10)
            w3 = wmm.rearrange("p (h t) -> p h t", h=4)
            nc.gpsimd.affine_select(out=w3, in_=w3, compare_op=ALU.is_ge, fill=0.0, base=0,
                                    pattern=[[0, 4], [1, P]], channel_multiplier=-1).then_inc(zeroed, 1)
            pool.wait_ge(zeroed, 7)
            nc.gpsimd.affine_select(out=wsb[:], in_=wsb[:], compare_op=ALU.is_ge, fill=0.0, base=0,
                                    pattern=[[0, 4], [1, TS]], channel_multiplier=-1).then_inc(zeroed, 1)
            pool.wait_ge(factor_half, 2)
            pool.wait_ge(y_scaled, KT)
            for k in range(NV_OUT, KT):
                nc.gpsimd.tensor_tensor(trunk[:, k, :], trunk[:, k, :], rstd[:], ALU.mult).then_inc(out_p, 1)

        @block.scalar
        def _(act):
            own, took = Count(), Count()

            def chain(ins):
                ins.then_inc(a_own, 1)
                act.wait_ge(a_own, own.up())

            def take():
                act.wait_ge(v_to_a, took.up())

            def split_hi(c, slot):
                act.wait_ge(w_landed[slot % RAW], landed(c, slot))
                if not isinstance(c, int) or c >= 6:
                    act.wait_ge(chunk_done, c - 3)
                nc.scalar.copy(w_hi[:, slot % RING, :], w_raw[:, slot % RAW, :]).then_inc(hi_ready, 1)

            act.wait_ge(zeroed, 1)
            nc.scalar.copy(cst[0:1, 0, 0:1], cst[0:1, 0, 0:1])
            act.wait_ge(consts_in, 16)
            act.wait_ge(alr_w_in, 16)
            act.wait_ge(zeroed, 2)
            nc.scalar.copy(alw[:, :, 0:RANK], al_raw.rearrange("p (k m) -> p k m", k=KT)).then_inc(alr_hi, 1)
            for k in range(KT):
                act.wait_ge(x_in[k // 2], 16)
                nc.scalar.mul(op_hi[:, k, :], trunk[:, k, :], vec[:, V_G1 + k:V_G1 + k + 1]).then_inc(op_h, 1)
                if k in SPLIT_AT:
                    split_hi(SPLIT_AT[k], SPLIT_AT[k])
            act.wait_ge(alr_w, 1)
            for k in range(KT):
                if k >= 2:
                    act.wait_ge(sq_add, k - 1)
                nc.scalar.activation(tmp[:, k % 2, :], trunk[:, k, :], ACT.Square).then_inc(sq_done, 1)

            def early(out, src):
                nc.scalar.copy(two(out), src).then_inc(acc_free, 1)

            def silu(i):
                take()
                nc.scalar.activation(tmp[:, i % 2, :], tmp[:, i % 2, :], ACT.Silu).then_inc(silu_r, 1)

            def out_squares(h):
                for e in range(2):
                    nc.scalar.activation(osq[:, e, :], mix[:, 2 * h + e, :], ACT.Square).then_inc(osq_a, 1)

            def post(kind, i):
                act.wait_ge(inter, number((kind, i)))
                last = None
                if kind == "var1":
                    last = nc.scalar.activation(two(rstd[:]), g01[:, :, 0:TH], ACT.Sqrt, bias=EPS, scale=1.0 / D)
                elif kind == "z":
                    js = range(4) if i == 0 else (4,)
                    rows = P if i == 0 else TS
                    for j in js:
                        last = nc.scalar.activation(loga[0:rows, j, :], g[j % 4][0:rows, :], ACT.Abs)
                    chain(last)
                    for j in js:
                        last = nc.scalar.activation(loga[0:rows, j, :], loga[0:rows, j, :], ACT.Exp, scale=-1.0)
                    chain(last)
                    for j in js:
                        last = nc.scalar.activation(loga[0:rows, j, :], loga[0:rows, j, :], ACT.Ln, bias=1.0)
                        if j < 3:
                            last.then_inc(a_to_v, 1)
                elif kind == "b":
                    w = 4 * (P if i < 4 else TS)
                    nc.scalar.activation(ex_p[:, 0:w], g[0][:, 0:w], ACT.Exp).then_inc(a_to_v, 1)
                    nc.scalar.activation(ex_n[:, 0:w], g[0][:, 0:w], ACT.Exp, scale=-1.0).then_inc(a_to_v, 1)
                    take()
                    last = nc.scalar.activation(ex_g[:, 0:w], ex_g[:, 0:w], ACT.Exp)
                elif kind == "mu":
                    for h in range(4):
                        take()
                        if h >= 2:
                            act.wait_ge(cm_add, h - 1)
                        last = nc.scalar.activation(tmp[:, h % 2, :], mix[:, 12 + h, :], ACT.Square)
                        if h < 3:
                            last.then_inc(cm_sq, 1)
                elif kind == "var_cm":
                    last = nc.scalar.activation(two(lnb), g23[:, :, 0:TH], ACT.Sqrt, bias=EPS, scale=1.0 / (4 * P))
                elif kind == "vvt":
                    act.wait_ge(post_v, parts(V_KINDS, ("var_cm", 0)))
                    act.dma_start(cmv, mix[:, 12:16, TP:T]).then_inc(cmv_out, 16)
                    nc.scalar.copy(vvt[:, 2, :], g[2])
                    last = nc.scalar.copy(vvt[:, 3, :], g[3])
                elif kind == "p":
                    last = nc.scalar.copy(mix[:, 0:8, P * i:P * (i + 1)],
                                          g01[:].rearrange("p a (s t) -> p (a s) t", s=4))
                elif kind == "s":
                    if i == 1:
                        nc.scalar.copy(vs4[0:TS, :], vs[:])
                        nc.scalar.copy(vs4[2 * TS:3 * TS, :], vs[:]).then_inc(a_to_v, 1)
                        last = nc.scalar.copy(mix[:, 0:8, TP:T], g[0][:, 0:8 * TS].rearrange("p (s t) -> p s t", s=8))
                elif kind == "on":
                    last = nc.scalar.activation(two(orstd), g01[:, :, 0:TH], ACT.Sqrt, bias=EPS, scale=1.0 / DV)
                if last is None:
                    last = act.nop()
                last.then_inc(post_a, 1)
                if kind == "on" and i < 3:
                    out_squares(i + 1)

            def evac(t):
                if T_CV <= t < T_V:
                    j = t - T_CV
                    take()
                    m = mix[:, 12 + j if t < T_CU else 4 + j, :]
                    nc.scalar.activation(m, m, ACT.Gelu).then_inc(gelu_done, 1)
                elif t >= T_R:
                    silu(t - T_R)

            def op_hi_tile(k):
                act.wait_ge(mix_done, 8 if k < 8 else k + 1)
                nc.scalar.copy(op_hi[:, k, :], mix[:, osl(k), :]).then_inc(op_h, 1)

            for c in range(2, C_OUT):
                act.wait_ge(chunk_done, c + 1)
                if c == C_OUT - 1:
                    evac(c // 2)
                    for k in range(HK, KT):
                        op_hi_tile(k)
                    split_hi(c + 4, c + 4)
                    continue
                if c == 3:
                    early(alr[0:2 * RANK, :], g23[0:2 * RANK, :, 0:TH])
                    early(qT[:, 0, :], accv(1))
                if c == 5:
                    early(qT[:, 1, :], accv(2))
                if c % 2 and c > 5:
                    evac(c // 2)
                for kind, i in plan.get(c, ()):
                    if kind in A_KINDS:
                        post(kind, i)
                if c == OSQ_AT:
                    act.wait_ge(post_v, parts(V_KINDS, ("s", 9)))
                    act.wait_ge(post_v, parts(V_KINDS, ("p", PAIRS - 1)))
                    out_squares(0)
                split_hi(c + 4, c + 4)
                if c == C_OUT - 2:
                    for k in range(HK):
                        op_hi_tile(k)

            def gfs(i, odd):
                if isinstance(i, int):
                    return vec[:, V_GF + 2 * i + odd:V_GF + 2 * i + odd + 1]
                return vec[:, bass.ds(i * 2 + (V_GF + odd), 1)]

            def square_h(m, par, base):
                act.wait_ge(hsq_add, m + (base[1] - 1))
                act.wait_ge(h_done, m + (base[0] + 1))
                nc.scalar.activation(tmp[:, par, :], trunk[:, m, :], ACT.Square).then_inc(hsq_done, 1)

            def sqrt_var(n):
                act.wait_ge(var_done, n)
                nc.scalar.activation(two(rstd[:]), g01[:, :, 0:TH], ACT.Sqrt, bias=EPS, scale=1.0 / D)\
                    .then_inc(std_done, 1)

            def op_hi_h(ks):
                for k in ks:
                    act.wait_ge(h_done, k + 1)
                    nc.scalar.mul(op_hi[:, k, :], trunk[:, k, :], vec[:, V_G2 + k:V_G2 + k + 1]).then_inc(op_h, 1)

            def out_tiles(i, tail):
                for s in range(4):
                    c = i * 4 + (C_OUT + s)
                    act.wait_ge(chunk_done, c + 1)
                    if s % 2:
                        square_h(i * 2 + s // 2, s // 2, (0, 2))
                    if tail and s == 3:
                        op_hi_h(range(HK, KT))
                    split_hi(c + 4, C_OUT + s + 4)
                    if tail and s == 2:
                        op_hi_h(range(HK))

            with act.Fori(0, KT // 2 - 1) as i:
                out_tiles(i, False)
            out_tiles(KT // 2 - 1, True)
            sqrt_var(1)

            def group(gr, last):
                with act.Fori(0, FG) as f:
                    for s in range(4):
                        c = gr * C_GRP + f * 4 + (C_FF + s)
                        act.wait_ge(chunk_done, c + 1)
                        if s == 1:
                            act.wait_ge(acc_free, gr * (C_GRP // 2) + f * 2 + (C_FF // 2 + 1))
                            nc.scalar.activation(tmp[:, 1, :], tmp[:, 1, :], ACT.Silu).then_inc(gate_act, 1)
                        if s == 3:
                            act.wait_ge(hid_f, gr * FG + f + 1)
                            nc.scalar.copy(hid_hi[:, f, :], tmp[:, 0, :]).then_inc(hid_h, 1)
                        split_hi(c + 4, C_FF + s + 4)

                def down(i, tail):
                    for s in range(4):
                        c = gr * C_GRP + i * 4 + (C_FF + C_GU + s)
                        act.wait_ge(chunk_done, c + 1)
                        if last and s % 2:
                            m = i * 2 + s // 2
                            square_h(m, s // 2, (KT, 20))
                            nc.scalar.mul(trunk[:, m, :], trunk[:, m, :], gfs(i, s // 2)).then_inc(y_scaled, 1)
                        if not tail:
                            split_hi(c + 4, C_FF + s + 4)

                with act.Fori(0, KT // 2 - (1 if last else 0)) as i:
                    down(i, False)
                if last:
                    down(KT // 2 - 1, True)

            with act.Fori(0, GROUPS - 1) as gr:
                group(gr, False)
            group(GROUPS - 1, True)
            sqrt_var(2)
            for a in range(2):
                act.wait_ge(factor_half, a + 1)
                nc.scalar.copy(g23[:, a, 0:TH], rstd[:, a * TH:(a + 1) * TH]).then_inc(factor_psum, 1)

        @block.tensor
        def _(pe):
            def products(t, slot, j, k, start, stop, rhs_hi, rhs_lo):
                w_h = w_hi[:, slot % RING, j * P:(j + 1) * P]
                w_l = w_lo[:, slot % RING, j * P:(j + 1) * P]
                for n, (w, x) in enumerate(((w_h, rhs_hi), (w_h, rhs_lo), (w_l, rhs_hi))):
                    for a in range(2):
                        last = nc.tensor.matmul(acc[t % 2][:, a, 0:TH], w, x[:, k, a * TH:(a + 1) * TH],
                                                start=start and n == 0, stop=stop and n == 2)
                return last

            def chunk(c, slot, t, par, ks, start, stop, rhs_hi=op_hi, rhs_lo=op_lo, ready=None):
                pe.wait_ge(hi_ready, c - 1)
                pe.wait_ge(lo_ready, c - 1)
                if start and not isinstance(t, int) or start and t > 2:
                    pe.wait_ge(acc_free, t - 1)
                for j, k in enumerate(ks):
                    if ready is not None:
                        ready(k)
                    last = products(par, slot, j, k, start and j == 0, stop and j == len(ks) - 1, rhs_hi, rhs_lo)
                last.then_inc(chunk_done, 1)

            pe.wait_ge(alr_w, 1)
            for k in range(KT):
                pe.wait_ge(op_rdy, k + 1)
                for n, x in enumerate((op_hi, op_lo)):
                    for a in range(2):
                        mm = nc.tensor.matmul(g23[:, a, 0:TH], alw[:, k, :], x[:, k, a * TH:(a + 1) * TH],
                                              start=(k == 0 and n == 0), stop=(k == KT - 1 and n == 1))
                        if k == KT - 1 and n == 1:
                            mm.then_inc(chunk_done, 1)
                if k % HK == 0:
                    pe.wait_ge(hi_ready, 1 + k // HK)
                    pe.wait_ge(lo_ready, 1 + k // HK)
                mm = products(1, 2 + k // HK, k % HK, k, k == 0, k == KT - 1, op_hi, op_lo)
                if k % HK == HK - 1:
                    mm.then_inc(chunk_done, 1)

            def ones_product(out2, buf):
                for a in range(2):
                    last = nc.tensor.matmul(out2[:, a, 0:TH], onesf[:], buf[:, a * TH:(a + 1) * TH],
                                            start=True, stop=True)
                return last

            def kd_transposes(i):
                w = P if i < 4 else TS
                for h in range(HEADS):
                    last = nc.tensor.transpose(g[1][0:w, h * P:(h + 1) * P], ex_g[:, h * w:(h + 1) * w], idn[:])
                return last

            def scores(i):
                for h in range(HEADS):
                    for r in (0, CHUNK):
                        tok = slice(i * P + r, i * P + r + CHUNK)
                        nc.tensor.matmul(g[2][r:r + CHUNK, h * P + r:h * P + r + CHUNK], kT[:, h, tok],
                                         qT[:, h, tok], start=True, stop=True)
                    nc.tensor.matmul(g[2][0:CHUNK, h * P + CHUNK:(h + 1) * P], ex_p[:, h * P:h * P + CHUNK],
                                     qT[:, h, i * P + CHUNK:(i + 1) * P], start=True, stop=True)

            def piece(kind, i):
                n = number((kind, i))
                before = order[:n - 1]
                if any(p[0] in V_KINDS for p in before):
                    pe.wait_ge(post_v, sum(p[0] in V_KINDS for p in before))
                if any(p[0] in A_KINDS for p in before):
                    pe.wait_ge(post_a, sum(p[0] in A_KINDS for p in before))
                if kind == "var1":
                    pe.wait_ge(zeroed, 6)
                    pe.wait_ge(sq_add, KT)
                    last = ones_product(g01, rstd[:])
                elif kind == "z":
                    pe.wait_ge(mid_in, 16 * 10)
                    for j in (range(4) if i == 0 else (4,)):
                        rows = P if j < 4 else TS
                        last = nc.tensor.matmul(g[j % 4][0:rows, :], alr[:, j * P:j * P + rows], wa2s,
                                                start=True, stop=True)
                elif kind == "b":
                    if i == 0:
                        pe.wait_ge(acc_free, T_CV)
                    if i >= 1:
                        kd_transposes(i - 1)
                        scores(i - 1)
                    w, tr = (P, triu[:, 0:P]) if i < 4 else (TS, triu[0:TS, P:P + TS])
                    for h in range(HEADS):
                        last = nc.tensor.matmul(g[0][:, h * w:(h + 1) * w], loga[0:w, i, h * P:(h + 1) * P], tr,
                                                start=True, stop=True)
                elif kind == "kdt":
                    last = kd_transposes(4)
                elif kind == "mu":
                    pe.wait_ge(gelu_done, 4)
                    for a in range(2):
                        for h in range(4):
                            last = nc.tensor.matmul(g23[:, a, 0:TH], onesf[:], mix[:, 12 + h, a * TH:(a + 1) * TH],
                                                    start=(h == 0), stop=(h == 3))
                elif kind == "var_cm":
                    last = ones_product(g23, lnb)
                elif kind == "vvt":
                    for j in range(4):
                        for h in range(4):
                            last = nc.tensor.transpose(g[j][:, h * P:(h + 1) * P],
                                                       mix[:, 12 + h, j * P:(j + 1) * P], idn[:])
                elif kind == "zc":
                    if i == 0:
                        pe.wait_ge(zeroed, 8)
                        for h in range(4):
                            nc.tensor.transpose(g[0][0:TS, h * P:(h + 1) * P], mix[:, 12 + h, TP:T], idn[:])
                    for h in (range(3) if i == 0 else (3,)):
                        for j in range(4):
                            last = nc.tensor.matmul(g[(h + 1) % 4][:, j * P:(j + 1) * P], vvt[:, j, h * P:(h + 1) * P],
                                                    wmm[:, h * P:(h + 1) * P], start=True, stop=True)
                    if i == 1:
                        for h in range(4):
                            last = nc.tensor.matmul(g[1][:, h * TS:(h + 1) * TS], vvts[:, h * P:(h + 1) * P],
                                                    wsb[:, h, :], start=True, stop=True)
                elif kind == "vt":
                    pe.wait_ge(acc_free, T_V + i + 1)
                    for j in range(4):
                        nc.tensor.transpose(g[2][:, j * P:(j + 1) * P], tmp[:, i % 2, j * P:(j + 1) * P], idn[:])
                    last = nc.tensor.transpose(g[3][0:TS, 0:P], tmp[:, i % 2, TP:T], idn[:])
                elif kind == "p":
                    tok = slice(P * i, P * (i + 1))
                    for h in range(HEADS):
                        for e in range(2):
                            out = g[h // 2][:, (2 * (h % 2) + e) * P:(2 * (h % 2) + e + 1) * P]
                            nc.tensor.matmul(out, v[:, i, h * DV + e * P:h * DV + (e + 1) * P], AT[:, h, tok],
                                             start=True, stop=(i == 0))
                            if i > 0:
                                nc.tensor.matmul(out, S[:, h, e * P:(e + 1) * P], qT[:, h, tok],
                                                 start=False, stop=True)
                    for h in range(HEADS):
                        last = nc.tensor.matmul(g[2 + h // 2][:, (h % 2) * DV:(h % 2 + 1) * DV],
                                                kd[:, i, h * P:(h + 1) * P], v[:, i, h * DV:(h + 1) * DV],
                                                start=True, stop=True)
                elif kind == "s":
                    for h in range(HEADS) if i < 2 else ():
                        if i == 0:
                            last = nc.tensor.matmul(g[0][0:TS, h * TS:(h + 1) * TS], kT[:, h, TP:T], qT[:, h, TP:T],
                                                    start=True, stop=True)
                        else:
                            for e in range(2):
                                last = nc.tensor.matmul(g[0][:, (2 * h + e) * TS:(2 * h + e + 1) * TS],
                                                        vs[0:TS, h * DV + e * P:h * DV + (e + 1) * P],
                                                        ATs[:, h * TS:(h + 1) * TS], start=True, stop=True)
                    if i >= 2:
                        n = i - 2
                        h, half = n // 2, n % 2
                        pe.wait_ge(s0_in[n % 2], 16 * (n // 2 + 1))
                        for e in range(2):
                            for b in range(4):
                                col = TP + DS * (4 * half + b)
                                nc.tensor.matmul(g[0][:, e * 16 + b * DS:e * 16 + (b + 1) * DS],
                                                 S0[:, n % 2, b * DV + e * P:b * DV + (e + 1) * P],
                                                 qT[:, h, col:col + DS], start=True, stop=True)
                        for b in range(4):
                            last = nc.tensor.matmul(g[2 + b // 2][:, (b % 2) * DV:(b % 2 + 1) * DV], kdm[:, b, :],
                                                    vs4[:, h * DV:(h + 1) * DV], start=True, stop=True)
                elif kind == "on":
                    pe.wait_ge(osq_rdy, i + 1)
                    last = ones_product(g01, osq[:, 0, :])
                last.then_inc(inter, 1)

            for c in range(3, C_OUT):
                if c > 3:
                    t, half = c // 2, c % 2
                    chunk(c, c, t, t, range(HK * half, HK * (half + 1)), half == 0, half == 1)
                for kind, i in plan.get(c, ()):
                    piece(kind, i)

            def op_ready(base):
                def ready(k):
                    if k % 2 == 0:
                        pe.wait_ge(op_rdy, base + k + 2)
                return ready

            with pe.Fori(0, KT // 2) as i:
                for s in range(4):
                    half = s % 2
                    chunk(i * 4 + (C_OUT + s), C_OUT + s, i * 2 + (N_IN + s // 2), N_IN + s // 2,
                          range(HK * half, HK * (half + 1)), half == 0, half == 1,
                          ready=op_ready(KT) if s < 2 else None)

            def sum_squares(n_add):
                pe.wait_ge(hsq_add, n_add)
                ones_product(g01, rstd[:]).then_inc(var_done, 1)

            def gate_up(gr, f, first=False):
                for s in range(4):
                    half = s % 2
                    chunk(gr * C_GRP + f * 4 + (C_FF + s), C_FF + s,
                          gr * (C_GRP // 2) + f * 2 + (C_FF // 2 + s // 2), C_FF // 2 + s // 2,
                          range(HK * half, HK * (half + 1)), half == 0, half == 1,
                          ready=op_ready(2 * KT) if first and s < 2 else None)
                    if first and s == 0:
                        sum_squares(2 + KT)

            def down(gr):
                def hid_ready(k):
                    if k == 0:
                        pe.wait_ge(hid_rdy, gr * FG + (FG - 1))
                    if k == FG - 1:
                        pe.wait_ge(hid_rdy, gr * FG + FG)

                with pe.Fori(0, KT // 2) as i:
                    for s in range(4):
                        half = s % 2
                        chunk(gr * C_GRP + i * 4 + (C_FF + C_GU + s), C_FF + s,
                              gr * (C_GRP // 2) + i * 2 + ((C_FF + C_GU) // 2 + s // 2), (C_FF + C_GU) // 2 + s // 2,
                              range(DA * half, DA if half == 0 else FG), half == 0, half == 1,
                              hid_hi, hid_lo, ready=hid_ready)

            gate_up(0, 0, first=True)
            with pe.Fori(1, FG) as f:
                gate_up(0, f)
            down(0)
            with pe.Fori(1, GROUPS) as gr:
                with pe.Fori(0, FG) as f:
                    gate_up(gr, f)
                down(gr)
            pe.wait_ge(hsq_add, 20 + KT - 1)
            for a in range(2):
                nc.tensor.matmul(g01[:, a, 0:TH], onesf[:], rstd[:, a * TH:(a + 1) * TH], start=True, stop=False)
            pe.wait_ge(hsq_done, 2 * KT)
            for a in range(2):
                last = nc.tensor.matmul(g01[:, a, 0:TH], onesf[:], tmp[:, (KT - 1) % 2, a * TH:(a + 1) * TH],
                                        start=False, stop=True)
            last.then_inc(var_done, 1)

        @block.vector
        def _(dve):
            own, took, freed = Count(), Count(), Count()

            def chain(ins):
                ins.then_inc(v_own, 1)
                dve.wait_ge(v_own, own.up())

            def take():
                dve.wait_ge(a_to_v, took.up())

            def f32(ap):
                return ap.bitcast(F32)

            def split_lo(c, slot):
                dve.wait_ge(hi_ready, c - 1)
                nc.vector.tensor_tensor(w_lo[:, slot % RING, :], w_raw[:, slot % RAW, :],
                                        f32(w_hi[:, slot % RING, :]), ALU.subtract).then_inc(lo_ready, 1)

            def op_lo_scaled(k, n, gcol):
                dve.wait_ge(op_h, n)
                nc.vector.scalar_tensor_tensor(out=op_lo[:, k, :], in0=trunk[:, k, :], scalar=vec[:, gcol:gcol + 1],
                                               in1=f32(op_hi[:, k, :]), op0=ALU.mult, op1=ALU.subtract)\
                    .then_inc(op_rdy, 1)

            dve.wait_ge(alr_hi, 1)
            nc.vector.tensor_tensor(alw[:, :, RANK:2 * RANK], al_raw.rearrange("p (k m) -> p k m", k=KT),
                                    f32(alw[:, :, 0:RANK]), ALU.subtract).then_inc(alr_w, 1)
            for k in range(KT):
                op_lo_scaled(k, k + 1, V_G1 + k)
                if k in SPLIT_AT:
                    split_lo(SPLIT_AT[k], SPLIT_AT[k])
            for k in range(KT):
                dve.wait_ge(sq_done, k + 1)
                if k == 0:
                    nc.vector.tensor_copy(rstd[:], tmp[:, 0, :]).then_inc(sq_add, 1)
                else:
                    dve.wait_ge(sq_add, k)
                    nc.vector.tensor_tensor(rstd[:], rstd[:], tmp[:, k % 2, :], ALU.add).then_inc(sq_add, 1)

            def normalised(out, src, rows=P):
                nc.vector.tensor_tensor(out, src[0:rows, :, 0:TH], two(rstd[0:rows, :]), ALU.mult)\
                    .then_inc(acc_free, 1)

            def kd_out(i):
                if i < 4:
                    return nc.vector.tensor_copy(kd[:, i, :], g[1])
                nc.vector.tensor_copy(kd4[0:TS, :], g[1][0:TS, :])
                chain(nc.vector.tensor_copy(kd4[TS:2 * TS, :], g[1][0:TS, :]))
                for q in (2, 3):
                    last = nc.vector.tensor_tensor(kd4[q * TS:(q + 1) * TS, :], g[1][0:TS, :], f32(kd4[0:TS, :]),
                                                   ALU.subtract)
                return last

            def decay(n):
                return egp[:, n, :].unsqueeze(2).to_broadcast([P, HEADS, CHUNK])

            def scores_out(i):
                tok = slice(i * P, (i + 1) * P)
                chain(nc.vector.memset(AT[:, :, tok], 0.0))
                sc = g[2].rearrange("p (h t) -> p h t", h=HEADS)
                m3 = mA[:].rearrange("p (h t) -> p h t", h=HEADS)
                for r in (0, CHUNK):
                    nc.vector.copy_predicated(AT[r:r + CHUNK, :, i * P + r:i * P + r + CHUNK], m3[r:r + CHUNK],
                                              sc[r:r + CHUNK, :, r:r + CHUNK])
                nc.vector.tensor_copy(AT[0:CHUNK, :, i * P + CHUNK:(i + 1) * P], sc[0:CHUNK, :, CHUNK:])
                q2 = qT[:, :, i * P + CHUNK:(i + 1) * P]
                nc.vector.tensor_tensor(q2, q2, decay(2 * i), ALU.mult)

            def mask_kd(n):
                h, half = n // 2, n % 2
                return nc.vector.tensor_tensor(kdm[:],
                                               f32(kd4[:, h * P:(h + 1) * P]).unsqueeze(1).to_broadcast([P, 4, P]),
                                               bm[:, 4 * half:4 * half + 4].unsqueeze(2).to_broadcast([P, 4, P]),
                                               ALU.mult)

            def out_square_sum(h):
                dve.wait_ge(osq_a, 2 * h + 2)
                nc.vector.tensor_tensor(osq[:, 0, :], osq[:, 0, :], osq[:, 1, :], ALU.add).then_inc(osq_rdy, 1)

            def post(kind, i):
                dve.wait_ge(inter, number((kind, i)))
                if kind == "var1":
                    dve.wait_ge(post_a, parts(A_KINDS, (kind, i)))
                    chain(nc.vector.reciprocal(rstd[:], rstd[:]))
                    dve.wait_ge(acc_free, 3)
                    nc.vector.tensor_tensor(alr[0:2 * RANK, :], alr[0:2 * RANK, :], rstd[0:2 * RANK, :], ALU.mult)
                    for h in range(2):
                        last = nc.vector.tensor_tensor(qT[:, h, :], qT[:, h, :], rstd[:], ALU.mult)
                elif kind == "z":
                    for j in (range(4) if i == 0 else (4,)):
                        rows = P if j < 4 else TS
                        if j < 3:
                            take()
                        else:
                            dve.wait_ge(post_a, parts(A_KINDS, (kind, i)))
                        last = nc.vector.scalar_tensor_tensor(out=loga[0:rows, j, :], in0=g[j % 4][0:rows, :],
                                                              scalar=0.0, in1=loga[0:rows, j, :],
                                                              op0=ALU.min, op1=ALU.subtract)
                elif kind == "b":
                    w = P if i < 4 else TS
                    n, lc = (2, CHUNK) if i < 4 else (DB, DS)
                    tok = slice(i * P, i * P + w)
                    if i >= 1:
                        kd_out(i - 1)
                        scores_out(i - 1)
                    take()
                    take()
                    chain(nc.vector.tensor_copy(ex_g[:, 0:4 * w], g[0][:, 0:4 * w]))
                    b4 = g[0][:, 0:4 * w].rearrange("p (a l) -> p a l", l=lc)
                    x4 = ex_g[:, 0:4 * w].rearrange("p (a l) -> p a l", l=lc)
                    nc.vector.tensor_tensor(x4, b4[:, :, lc - 1:lc].to_broadcast([P, HEADS * n, lc]), x4,
                                            ALU.subtract).then_inc(v_to_a, 1)
                    ends = ex_p[:, 0:4 * w].rearrange("p (h n l) -> p h n l", h=HEADS, n=n)[:, :, :, lc - 1]
                    dst = egp[:, 2 * i:2 * i + 2, :].rearrange("p n h -> p h n") if i < 4 else egs[:]
                    nc.vector.tensor_copy(dst, ends)

                    def heads(buf):
                        return buf[:, 0:4 * w].rearrange("p (h t) -> p h t", h=HEADS)

                    chain(nc.vector.scalar_tensor_tensor(out=qT[:, :, tok], in0=qT[:, :, tok], scalar=DK ** -0.5,
                                                         in1=heads(ex_p), op0=ALU.mult, op1=ALU.mult))
                    dve.wait_ge(post_a, parts(A_KINDS, (kind, i)))
                    if i < 4:
                        eg, first = heads(ex_g), heads(ex_p)[:, :, 0:CHUNK]
                        chain(nc.vector.tensor_tensor(first, kT[:, :, i * P:i * P + CHUNK], eg[:, :, 0:CHUNK], ALU.mult))
                        nc.vector.tensor_tensor(eg[:, :, 0:CHUNK], first, decay(2 * i + 1), ALU.mult)
                        chain(nc.vector.tensor_tensor(eg[:, :, CHUNK:], kT[:, :, i * P + CHUNK:(i + 1) * P],
                                                      eg[:, :, CHUNK:], ALU.mult))
                    else:
                        nc.vector.tensor_tensor(heads(ex_g), kT[:, :, tok], heads(ex_g), ALU.mult)
                    last = nc.vector.tensor_tensor(kT[:, :, tok], kT[:, :, tok], heads(ex_n), ALU.mult)
                elif kind == "kdt":
                    chain(kd_out(4))
                    nc.vector.tensor_tensor(egp[:, ::2, :], egp[:, ::2, :], egp[:, 1::2, :], ALU.mult)
                    last = mask_kd(0)
                elif kind == "mu":
                    dve.wait_ge(gelu_done, 4)
                    for h in range(4):
                        nc.vector.scalar_tensor_tensor(out=two(mix[:, 12 + h, :]), in0=g23[:, :, 0:TH],
                                                       scalar=-1.0 / (4 * P), in1=two(mix[:, 12 + h, :]),
                                                       op0=ALU.mult, op1=ALU.add).then_inc(v_to_a, 1)
                    for h in range(4):
                        if h < 3:
                            dve.wait_ge(cm_sq, h + 1)
                        else:
                            dve.wait_ge(post_a, parts(A_KINDS, (kind, i)))
                        if h == 0:
                            last = nc.vector.tensor_copy(lnb, tmp[:, 0, :])
                        else:
                            dve.wait_ge(cm_add, h)
                            last = nc.vector.tensor_tensor(lnb, lnb, tmp[:, h % 2, :], ALU.add)
                        if h < 3:
                            last.then_inc(cm_add, 1)
                elif kind == "var_cm":
                    dve.wait_ge(post_a, parts(A_KINDS, (kind, i)))
                    chain(nc.vector.reciprocal(lnb, lnb))
                    for h in range(4):
                        last = nc.vector.scalar_tensor_tensor(out=mix[:, 12 + h, :], in0=mix[:, 12 + h, :],
                                                              scalar=vec[:, V_LG + h:V_LG + h + 1], in1=lnb,
                                                              op0=ALU.mult, op1=ALU.mult)
                    chain(last)
                    for h in range(4):
                        last = nc.vector.tensor_scalar(mix[:, 12 + h, :], mix[:, 12 + h, :],
                                                       vec[:, V_LB + h:V_LB + h + 1], None, ALU.add)
                elif kind == "vvt":
                    nc.vector.tensor_copy(vvt[:, 0, :], g[0])
                    last = nc.vector.tensor_copy(vvt[:, 1, :], g[1])
                elif kind == "zc":
                    if i == 0:
                        nc.vector.tensor_copy(vvts[:], g[0][0:TS, :])
                    hs = range(3) if i == 0 else (3,)
                    for h in hs:
                        last = nc.vector.tensor_tensor(
                            mix[:, 12 + h, 0:TP].rearrange("p (j t) -> p j t", j=4),
                            g[(h + 1) % 4].rearrange("p (j t) -> p j t", j=4),
                            bsb[:, h * P:(h + 1) * P].unsqueeze(1).to_broadcast([P, 4, P]), ALU.add)
                    if i == 1:
                        dve.wait_ge(cmv_out, 16)
                        for h in range(4):
                            last = nc.vector.tensor_tensor(
                                mix[:, 12 + h, TP:T].rearrange("p (b t) -> p b t", b=DB),
                                g[1][:, h * TS:(h + 1) * TS].rearrange("p (b t) -> p b t", b=DB),
                                bsb[:, h * P:h * P + DS].unsqueeze(1).to_broadcast([P, DB, DS]), ALU.add)
                    if i == 1:
                        chain(last)
                        dve.wait_ge(gelu_done, 8)
                        for h in range(4):
                            last = nc.vector.tensor_tensor(mix[:, 12 + h, :], mix[:, 12 + h, :], mix[:, 8 + h, :],
                                                           ALU.mult)
                            last.then_inc(mix_done, 1)
                        dve.wait_ge(mix_done, 4)
                        last = None
                elif kind == "vt":
                    nc.vector.tensor_copy(v[:, 0:4, i * P:(i + 1) * P], g[2].rearrange("p (j e) -> p j e", j=4))
                    last = nc.vector.tensor_copy(vs[0:TS, i * P:(i + 1) * P], g[3][0:TS, 0:P])
                elif kind == "p":
                    for h in range(HEADS):
                        ds = g[2 + h // 2][:, (h % 2) * DV:(h % 2 + 1) * DV]
                        if i == 0:
                            last = nc.vector.tensor_copy(S[:, h, :], ds)
                        else:
                            last = nc.vector.scalar_tensor_tensor(out=S[:, h, :], in0=S[:, h, :],
                                                                  scalar=egp[:, 2 * i, h:h + 1], in1=ds,
                                                                  op0=ALU.mult, op1=ALU.add)
                elif kind == "s":
                    if i == 0:
                        last = nc.vector.copy_predicated(ATs[:], mS[:], g[0][0:TS, 0:HEADS * TS])
                    elif i == 1:
                        take()
                        for q in (1, 3):
                            last = nc.vector.tensor_tensor(vs4[q * TS:(q + 1) * TS, :], vs[:], f32(vs4[0:TS, :]),
                                                           ALU.subtract)
                    else:
                        n = i - 2
                        h, half = n // 2, n % 2
                        o = mix[:, 2 * h:2 * h + 2, TP + 16 * half:TP + 16 * (half + 1)]
                        nc.vector.tensor_tensor(o, g[0][:, 0:32].rearrange("p (e t) -> p e t", e=2), o, ALU.add)
                        if n + 1 < 8:
                            mask_kd(n + 1)
                        for b in range(4):
                            last = nc.vector.scalar_tensor_tensor(
                                out=S0[:, n % 2, b * DV:(b + 1) * DV], in0=S0[:, n % 2, b * DV:(b + 1) * DV],
                                scalar=egs[:, h, 4 * half + b:4 * half + b + 1],
                                in1=g[2 + b // 2][:, (b % 2) * DV:(b % 2 + 1) * DV], op0=ALU.mult, op1=ALU.add)
                elif kind == "on":
                    dve.wait_ge(post_a, parts(A_KINDS, (kind, i)))
                    chain(nc.vector.reciprocal(orstd, orstd))
                    if i < 3:
                        out_square_sum(i + 1)
                    for e in range(2):
                        m = 2 * i + e
                        last = nc.vector.scalar_tensor_tensor(out=mix[:, m, :], in0=mix[:, m, :],
                                                              scalar=vec[:, V_GLA + m:V_GLA + m + 1], in1=orstd,
                                                              op0=ALU.mult, op1=ALU.mult)
                if last is None:
                    last = dve.nop()
                last.then_inc(post_v, 1)

            zpp = zp[:, 0:2 + TP]
            zps = zp[:, 2 + TP:].rearrange("p (b t) -> p b t", b=DB)

            def conv_tile(i):
                nc.vector.tensor_tensor(zpp[:, 2:], tmp[:, 0, 0:TP], tmp[:, 1, 0:TP], ALU.mult)
                nc.vector.tensor_tensor(zps[:, :, 2:], tmp[:, 0, TP:T].rearrange("p (b t) -> p b t", b=DB),
                                        tmp[:, 1, TP:T].rearrange("p (b t) -> p b t", b=DB), ALU.mult)
                chain(nc.vector.tensor_copy(zps[:, :, 0:2], cbs[:, i, :].rearrange("p (b t) -> p b t", b=DB)))
                mp = mix[:, 8 + i, 0:TP]
                ms = mix[:, 8 + i, TP:T].rearrange("p (b t) -> p b t", b=DB)
                for z, m, n in ((zpp, mp, TP), (zps, ms, DS)):
                    def tap(j):
                        return z[:, j:j + n] if n == TP else z[:, :, j:j + n]
                    for j in range(3):
                        w = vec[:, V_CW + 4 * j + i:V_CW + 4 * j + i + 1]
                        if j == 0:
                            chain(nc.vector.tensor_scalar(m, tap(0), w, vec[:, V_CB + i:V_CB + i + 1],
                                                          ALU.mult, ALU.add))
                        else:
                            chain(nc.vector.scalar_tensor_tensor(out=m, in0=tap(j), scalar=w, in1=m,
                                                                 op0=ALU.mult, op1=ALU.add))
                nc.vector.tensor_copy(cst[:, i, 0:2], zpp[:, TP:TP + 2])
                nc.vector.tensor_copy(cst[:, i, 2:].rearrange("p (b t) -> p b t", b=DB), zps[:, :, DS:DS + 2])

            def evac(t):
                if t < T_CV:
                    normalised(two((qT if t < T_K else kT)[:, (t - T_Q) % 4, :]), acc[t % 2])
                elif t < T_V:
                    j = t - T_CV
                    m = mix[:, 12 + j if t < T_CU else 4 + j, :]
                    normalised(two(m), acc[t % 2])
                    dve.wait_ge(acc_free, t + 1)
                    dve.nop().then_inc(v_to_a, 1)
                elif t < T_CONV:
                    normalised(two(tmp[:, (t - T_V) % 2, :]), acc[t % 2])
                elif t < T_R:
                    i, part = divmod(t - T_CONV, 3)
                    if part == 0 and i >= 1:
                        dve.wait_ge(mix_done, 4 + i)
                    normalised(two(tmp[:, 1 if part == 1 else 0, :]), acc[t % 2])
                    if part >= 1:
                        dve.wait_ge(acc_free, t + 1)
                    if part == 1:
                        conv_tile(i)
                    if part == 2:
                        nc.vector.tensor_tensor(mix[:, 8 + i, :], mix[:, 8 + i, :], tmp[:, 0, :], ALU.mult)\
                            .then_inc(mix_done, 1)
                else:
                    i = t - T_R
                    normalised(two(tmp[:, i % 2, :]), acc[t % 2])
                    dve.wait_ge(acc_free, t + 1)
                    dve.nop().then_inc(v_to_a, 1)
                    dve.wait_ge(silu_r, i + 1)
                    nc.vector.tensor_tensor(mix[:, i, :], mix[:, i, :], tmp[:, i % 2, :], ALU.mult)\
                        .then_inc(mix_done, 1)

            def op_lo_tile(k):
                dve.wait_ge(op_h, KT + k + 1)
                nc.vector.tensor_tensor(op_lo[:, k, :], mix[:, osl(k), :], f32(op_hi[:, k, :]), ALU.subtract)\
                    .then_inc(op_rdy, 1)

            for c in range(2, C_OUT):
                dve.wait_ge(chunk_done, c + 1)
                if c == C_OUT - 1:
                    evac(c // 2)
                    for k in range(HK, KT):
                        op_lo_tile(k)
                    split_lo(c + 4, c + 4)
                    continue
                if c % 2 and c > 5:
                    evac(c // 2)
                for kind, i in plan.get(c, ()):
                    if kind in V_KINDS:
                        post(kind, i)
                if c == OSQ_AT:
                    out_square_sum(0)
                split_lo(c + 4, c + 4)
                if c == C_OUT - 2:
                    for k in range(HK):
                        op_lo_tile(k)

            def zero_sum(n_read):
                dve.wait_ge(acc_free, n_read)
                nc.vector.memset(rstd[:], 0.0).then_inc(hsq_add, 2)

            def residual(t, par, m, squares=None):
                dve.wait_ge(acc_free, t)
                nc.vector.tensor_tensor(two(trunk[:, m, :]), acc[par % 2][:, :, 0:TH], two(trunk[:, m, :]), ALU.add)\
                    .then_inc(acc_free, 1)
                if squares is not None:
                    h_base, add_base, skip = squares
                    dve.wait_ge(acc_free, t + 1)
                    dve.nop().then_inc(h_done, 1)
                    if skip:
                        return
                    dve.wait_ge(hsq_done, m + (h_base + 1))
                    dve.wait_ge(hsq_add, m + add_base)
                    nc.vector.tensor_tensor(rstd[:], rstd[:], tmp[:, par_of(m, par), :], ALU.add)\
                        .then_inc(hsq_add, 1)

            def par_of(m, par):
                return (par + 1) % 2

            def reciprocal_std(n):
                dve.wait_ge(std_done, n)
                nc.vector.reciprocal(rstd[:], rstd[:]).then_inc(rstd_ok, 1)

            zero_sum(N_IN)
            dve.wait_ge(x_back, 16 * 4)
            def out_tiles(i, tail):
                for s in range(4):
                    c = i * 4 + (C_OUT + s)
                    dve.wait_ge(chunk_done, c + 1)
                    if s % 2:
                        residual(i * 2 + (N_IN + s // 2), N_IN + s // 2, i * 2 + s // 2, (0, 2, False))
                    if tail and s == 3:
                        for k in range(HK, KT):
                            op_lo_scaled(k, 2 * KT + k + 1, V_G2 + k)
                    split_lo(c + 4, C_OUT + s + 4)
                    if tail and s == 2:
                        for k in range(HK):
                            op_lo_scaled(k, 2 * KT + k + 1, V_G2 + k)

            with dve.Fori(0, KT // 2 - 1) as i:
                out_tiles(i, False)
            out_tiles(KT // 2 - 1, True)
            reciprocal_std(1)

            def group(gr, last):
                with dve.Fori(0, FG) as f:
                    for s in range(4):
                        c = gr * C_GRP + f * 4 + (C_FF + s)
                        t = gr * (C_GRP // 2) + f * 2 + (C_FF // 2 + s // 2)
                        par = C_FF // 2 + s // 2
                        dve.wait_ge(chunk_done, c + 1)
                        if s == 1:
                            dve.wait_ge(rstd_ok, 1)
                            normalised(two(tmp[:, 1, :]), acc[par % 2])
                        if s == 3:
                            normalised(two(tmp[:, 0, :]), acc[par % 2])
                            dve.wait_ge(acc_free, t + 1)
                            dve.wait_ge(gate_act, gr * FG + f + 1)
                            nc.vector.tensor_tensor(tmp[:, 0, :], tmp[:, 0, :], tmp[:, 1, :], ALU.mult)\
                                .then_inc(hid_f, 1)
                            dve.wait_ge(hid_h, gr * FG + f + 1)
                            nc.vector.tensor_tensor(hid_lo[:, f, :], tmp[:, 0, :], f32(hid_hi[:, f, :]),
                                                    ALU.subtract).then_inc(hid_rdy, 1)
                        split_lo(c + 4, C_FF + s + 4)

                def down(i, tail):
                    for s in range(4):
                        c = gr * C_GRP + i * 4 + (C_FF + C_GU + s)
                        dve.wait_ge(chunk_done, c + 1)
                        if s % 2:
                            t0 = (C_FF + C_GU) // 2 + s // 2
                            residual(gr * (C_GRP // 2) + i * 2 + t0, t0, i * 2 + s // 2,
                                     (KT, 20, tail and s == 3) if last else None)
                        if not tail:
                            split_lo(c + 4, C_FF + s + 4)

                if last:
                    zero_sum(gr * (C_GRP // 2) + (C_FF + C_GU) // 2)
                with dve.Fori(0, KT // 2 - (1 if last else 0)) as i:
                    down(i, False)
                if last:
                    down(KT // 2 - 1, True)

            with dve.Fori(0, GROUPS - 1) as gr:
                group(gr, False)
            group(GROUPS - 1, True)
            dve.wait_ge(std_done, 2)
            for a in range(2):
                nc.vector.reciprocal(rstd[:, a * TH:(a + 1) * TH], rstd[:, a * TH:(a + 1) * TH])\
                    .then_inc(factor_half, 1)
            dve.wait_ge(y_scaled, KT)
            dve.wait_ge(factor_psum, 2)
            for k in range(NV_OUT):
                nc.vector.tensor_tensor(two(trunk[:, k, :]), two(trunk[:, k, :]), g23[:, :, 0:TH], ALU.mult)\
                    .then_inc(out_v, 1)


INS = ("xT", "w_alr", "w_in", "w_out", "w_gu", "w_da", "w_db", "vecs", "wa2", "wm", "wsbd", "bs", "s0", "cbuf",
       "ident", "tri", "maskA", "maskS", "bmask")
OUTS = (("yT", (P, KT, T)), ("gla_p", (HEADS, DK, DV)), ("gla_s", (HEADS, 2, P, 4 * DV)),
        ("conv_o", (P, 4, 2 + 2 * DB)), ("cmv", (P, 4, TS)))


def kernel(**inputs):
    import numpy as np
    import concourse.bacc as bacc
    from concourse.bass_utils import run_bass_kernel_spmd

    a = {k: np.asarray(x) for k, x in inputs.items()}

    def feature_major(x):
        return x.reshape(x.shape[0], -1, P).transpose(2, 1, 0)

    def tiles(w):
        k, m = w.shape
        return w.reshape(2, k // P // 2, P, m // P, P).transpose(3, 0, 2, 1, 4).reshape(m // P * 2, P, -1)

    x = np.concatenate([a["x_prompt"].reshape(TP, D), a["x_sample"].reshape(TS, D)])
    w = a["w_in"][0]
    parts, at = [], 0
    for n in (HEADS * DK, HEADS * DK, HEADS * DV, HEADS * DV, RANK, 512, 512, 512, 512, 512):
        parts.append(w[:, at:at + n])
        at += n
    wq, wk, wv, wr, wal, wcb, wcc, wch, wcu, wcv = parts
    conv = np.concatenate([y[:, i * P:(i + 1) * P] for i in range(4) for y in (wcc, wch, wcb)], axis=1)
    win = tiles(np.concatenate([wq, wk, wcv, wcu, wv, conv, wr], axis=1))
    wo = a["w_out"][0].reshape(KT, P, D)[MIX_ORDER].reshape(D, D)
    gu = np.stack([a["w_gate"][0].reshape(D, FT, P), a["w_up"][0].reshape(D, FT, P)], axis=2).reshape(D, 2 * DFF)
    wd = a["w_down"][0].reshape(GROUPS, FG, P, KT, P).transpose(0, 3, 2, 1, 4)
    cols = [feature_major(a[n].reshape(-1, size))[:, :, j] for n, size in
            (("norm1_g", D), ("norm2_g", D), ("final_g", D), ("gla_g", HEADS * DV), ("conv_w", 512), ("conv_b", 512),
             ("cm_ln_g", 512), ("cm_ln_b", 512)) for j in range(a[n].size // size)]
    ws = a["cm_ws"][0]
    wsbd = np.zeros((TS, 4, TS), ws.dtype)
    for b in range(DB):
        wsbd[b * DS:(b + 1) * DS, :, b * DS:(b + 1) * DS] = ws[:, :DS, :DS].transpose(2, 0, 1)
    s, t = np.arange(P)[:, None], np.arange(P)[None, :]
    tri = ((s <= t) & (s // CHUNK == t // CHUNK)) / 16.0
    tri_s = ((s <= t) & (s // DS == t // DS))[:, :TS] / 16.0
    arrays = {
        "xT": feature_major(x),
        "w_alr": wal.reshape(KT, P, RANK).transpose(1, 0, 2),
        "w_in": win,
        "w_out": tiles(wo),
        "w_gu": tiles(gu),
        "w_da": wd[:, :, :, :DA].reshape(GROUPS * KT, P, DA * P),
        "w_db": wd[:, :, :, DA:].reshape(GROUPS * KT, P, (FG - DA) * P),
        "vecs": np.concatenate(cols, axis=1),
        "wa2": np.concatenate([a["w_a2"][0], a["w_a2"][0], a["b_a"][:1]]),
        "wm": ws.transpose(2, 0, 1).reshape(P, 4 * P),
        "wsbd": wsbd,
        "bs": a["cm_bs"][0].reshape(4 * P),
        "s0": a["state_gla"][0].reshape(2, 4, HEADS, DK, DV).transpose(2, 0, 3, 1, 4).reshape(HEADS, 2, P, 4 * DV),
        "cbuf": a["state_conv"][0].reshape(2 * DB, 4, P).transpose(2, 1, 0),
        "ident": np.eye(P, dtype=np.float32),
        "tri": np.concatenate([tri, tri_s], axis=1).astype(np.float32),
        "maskA": np.tile(s % CHUNK <= t[:, :CHUNK], (1, HEADS)).astype(np.int32),
        "maskS": np.tile(((s <= t) & (s // DS == t // DS))[:TS, :TS], (1, HEADS)).astype(np.int32),
        "bmask": (s % TS // DS == t[:, :DB]).astype(np.float32),
    }
    arrays = {n: np.ascontiguousarray(y) for n, y in arrays.items()}
    nc = bacc.Bacc("TRN2", target_bir_lowering=False, num_devices=1, dynamic_dma_scratch_size=1024)
    args = [nc.dram_tensor(n, arrays[n].shape, mybir.dt.from_np(arrays[n].dtype), kind="ExternalInput").ap()
            for n in INS]
    args += [nc.dram_tensor(n, shape, F32, kind="ExternalOutput").ap() for n, shape in OUTS]
    build(nc, *args)
    r = run_bass_kernel_spmd(nc, [arrays], core_ids=[0]).results[0]
    y = r["yT"].transpose(2, 1, 0).reshape(T, D)
    cst = r["conv_o"].transpose(2, 1, 0).reshape(2 + 2 * DB, 512)
    gs = r["gla_s"].reshape(HEADS, 2, DK, 4, DV).transpose(1, 3, 0, 2, 4).reshape(1, DB, HEADS, DK, DV)
    return (y[:TP].reshape(1, TP, D), y[TP:].reshape(DB, DS, D), r["gla_p"].reshape(1, 1, HEADS, DK, DV),
            cst[:2].reshape(1, 1, 2, 512), gs, cst[2:].reshape(1, DB, 2, 512),
            r["cmv"].transpose(2, 1, 0).reshape(1, DB, DS, 512))
```

```python
from contextlib import ExitStack

import concourse.bass as bass
from concourse import mybir

F32 = mybir.dt.float32
F32R = mybir.dt.float32r
I32 = mybir.dt.int32
ALU = mybir.AluOpType
ACT = mybir.ActivationFunctionType

P = 128
D = 2048
KT = D // P
TP = 512
DB, DS = 8, 4
TS = DB * DS
T = TP + TS
QB = P + DS
TH = T // 2
HEADS, DK, DV, RANK = 4, 128, 256, 16
CHUNK = 64
NCHUNK = TP // CHUNK
PAIRS = NCHUNK // 2
DFF = 5632
FT = DFF // P
GROUPS = 4
FG = FT // GROUPS
EPS = 1e-6

T_Q, T_K, T_CV, T_CU, T_V, T_CONV, T_R, N_IN = 1, 5, 9, 13, 17, 25, 37, 45
HK = KT // 2
CH = HK * P
RING = 4
RAW = 2
C_OUT = 2 * N_IN
C_FF = C_OUT + 2 * KT
C_GU = 4 * FG
C_GRP = C_GU + 2 * KT
DA = (FG + 1) // 2
MIX_ORDER = list(range(HK, KT)) + list(range(HK))

VAR1_AT = 6
Z_AT = (8, 11)
B_AT = (19, 21, 23, 25, 27)
KDT_AT = 29
MU_AT, VAR_CM_AT, VVT_AT, ZC_AT = 28, 31, 34, (36, 38)
VT_AT = tuple(37 + 2 * i for i in range(8))
P_AT = (53, 57, 61, 65)
QS_AT = tuple(42 + i for i in range(8))
S_AT = tuple(50 + 2 * i for i in range(10))
OSQ_AT = 69
ON_AT = (71, 73, 75, 77)

BLOCKS = tuple((a * TH + at, skip, w) for a in range(2)
               for at, skip, w in ((0, 0, P), (P, 0, P), (TH - P, 3 * P - TH, TH - 2 * P)))
WARM = 14
NV_OUT = 12
OUT_ORDER = (2, 4, 6, 12, 8, 14, 10)
SPLIT_AT = {1: 2, 3: 3, 10: 4, 15: 5}

V_G1, V_G2, V_GF, V_GLA, V_CW, V_CB, V_LG, V_LB, NV = 0, 16, 32, 48, 56, 68, 72, 76, 80

NORM_2, NORM_F = (0, 2), (KT, 2 + KT + 2)

A_KINDS = ("var1", "z", "b", "mu", "var_cm", "vvt", "p", "s", "on")
V_KINDS = A_KINDS + ("kdt", "zc", "vt", "qs")


def mixer_plan():
    plan = {}
    for kind, places in (("var1", (VAR1_AT,)), ("z", Z_AT), ("b", B_AT), ("kdt", (KDT_AT,)), ("mu", (MU_AT,)),
                         ("var_cm", (VAR_CM_AT,)), ("vvt", (VVT_AT,)), ("zc", ZC_AT), ("vt", VT_AT), ("qs", QS_AT),
                         ("p", P_AT), ("s", S_AT), ("on", ON_AT)):
        for i, c in enumerate(places):
            plan.setdefault(c, []).append((kind, i))
    order = [piece for c in sorted(plan) for piece in plan[c]]
    return plan, order


class Count:

    def __init__(self):
        self.n = 0

    def up(self):
        self.n += 1
        return self.n


def build(nc, xT, w_alr, w_in, w_out, w_gu, w_da, w_db, vecs, wa2, wm, wsbd, bs, s0, cbuf, ident, tri, maskA, maskS,
          bmask, yT, gla_p, gla_s, conv_o, cmv):
    with ExitStack() as ctx:
        def sb(name, shape, dt=F32):
            return ctx.enter_context(nc.sbuf_tensor(name, shape, dt))

        def sem(name):
            return ctx.enter_context(nc.semaphore(name))

        trunk = sb("trunk", [P, KT, T])
        op_hi = sb("op_hi", [P, KT, T], F32R)
        op_lo = sb("op_lo", [P, KT, T], F32R)
        w_raw = sb("w_raw", [P, RAW, CH])
        w_hi = sb("w_hi", [P, RING, CH], F32R)
        w_lo = sb("w_lo", [P, RING, CH], F32R)
        vec = sb("vec", [P, NV])
        idn = sb("idn", [P, P])
        onesf = sb("onesf", [P, P])
        rstd = sb("rstd", [P, T])
        tmp = sb("tmp", [P, 2, T])
        one = sb("one", [1, 1])
        cst = sb("cst", [P, 4, 2 + 2 * DB])
        with ExitStack() as ff:
            hid_hi = ff.enter_context(nc.sbuf_tensor("hid_hi", [P, FG, T], F32R))
            hid_lo = ff.enter_context(nc.sbuf_tensor("hid_lo", [P, FG, T], F32R))
        with ExitStack() as states:
            s0_hi = states.enter_context(nc.sbuf_tensor("s0_hi", [P, 2, 4 * DV], F32R))
            s0_lo = states.enter_context(nc.sbuf_tensor("s0_lo", [P, 2, 4 * DV], F32R))
            qm = states.enter_context(nc.sbuf_tensor("qm", [P, DB * QB + TS], F32R))
        mix = sb("mix", [P, KT, T])
        kd = sb("kd", [P, 4, HEADS * DK])
        ov = sb("ov", [3 * TS, HEADS * DV])
        vs4 = sb("vs4", [P, HEADS * DV], F32R)
        kd4 = sb("kd4", [P, HEADS * DK], F32R)
        S = sb("S", [P, HEADS, DV])
        with nc.sbuf_tensor("alw", [P, KT, P], F32R) as alw:
            pass
        S0 = sb("S0", [P, 2, 4 * DV])
        kdm = sb("kdm", [P, 4, DK], F32R)
        ovm = sb("ovm", [3 * TS, HEADS * TS])
        triu = sb("triu", [P, P + TS])
        mA = sb("mA", [P, HEADS * CHUNK], I32)
        mS = sb("mS", [3 * TS, HEADS * TS], I32)
        bm = sb("bm", [P, DB])
        egp = sb("egp", [P, NCHUNK, HEADS])
        egs = sb("egs", [P, HEADS, DB])
        wsb = sb("wsb", [32, 4, TS])
        zp = sb("zp", [P, 2 + TP + DB * (2 + DS)])
        cbs = sb("cbs", [P, 4, 2 * DB])
        o_tok, vs, ATs = ov[0:2 * TS], ov[2 * TS:], ovm[2 * TS:]
        trf = trunk[:].rearrange("p k t -> p (k t)")
        qT = trf[:, 0:HEADS * T].rearrange("p (h t) -> p h t", h=HEADS)
        kT = trf[:, HEADS * T:2 * HEADS * T].rearrange("p (h t) -> p h t", h=HEADS)
        AT = kT
        v = trf[:, 2 * HEADS * T:2 * HEADS * T + 4 * HEADS * DV].rearrange("p (j e) -> p j e", j=4)
        mxf = mix[:].rearrange("p k t -> p (k t)")
        loga = mxf[:, 0:5 * 512].rearrange("p (j d) -> p j d", j=5)
        ex_g, ex_p, ex_n = (mxf[:, (5 + i) * 512:(6 + i) * 512] for i in range(3))
        vvts = mxf[0:TS, 5 * 512:6 * 512]
        vvt = S0[:].rearrange("p a (b c) -> p (a b) c", b=2)
        wmm = S[:].rearrange("p h e -> p (h e)")[:, 0:512]
        bsb = S[:].rearrange("p h e -> p (h e)")[:, 512:1024]
        kdf = kd[:].rearrange("p j d -> p (j d)")
        alr = kdf[0:2 * RANK + 1, 0:T]
        wa2s = kdf[0:2 * RANK + 1, T:T + HEADS * DK]
        lnb = zp[:, 2:2 + T]
        osq = kdf[:, 0:2 * T].rearrange("p (a t) -> p a t", a=2)
        orstd = kdf[:, 2 * T:3 * T]
        colf = vec[:, V_G1:V_G1 + len(BLOCKS)]
        diag = tmp[:].rearrange("p a t -> p (a t)")[:, 0:len(BLOCKS) * P]
        al_raw = tmp[:].rearrange("p a t -> p (a t)")[:, 0:KT * RANK]
        acc = [ctx.enter_context(nc.psum_tensor(f"acc{i}", [P, 2, 512], F32)) for i in range(2)]
        g01 = ctx.enter_context(nc.psum_tensor("g01", [P, 2, 512], F32))
        g23 = ctx.enter_context(nc.psum_tensor("g23", [P, 2, 512], F32))
        g = [g01[:, 0, :], g01[:, 1, :], g23[:, 0, :], g23[:, 1, :]]

        def accv(t):
            return acc[t % 2][:, :, 0:TH]

        def two(ap):
            return ap.rearrange("p (a t) -> p a t", a=2)

        consts_in = sem("consts_in")
        alr_w_in = sem("alr_w_in")
        mid_in = sem("mid_in")
        x_in = [sem(f"x_in{i}") for i in range(8)]
        w_landed = [sem(f"w_landed{i}") for i in range(RAW)]
        hi_ready = sem("hi_ready")
        lo_ready = sem("lo_ready")
        zeroed = sem("zeroed")
        alr_hi = sem("alr_hi")
        alr_w = sem("alr_w")
        op_h = sem("op_h")
        op_rdy = sem("op_rdy")
        sq_done = sem("sq_done")
        sq_add = sem("sq_add")
        chunk_done = sem("chunk_done")
        acc_free = sem("acc_free")
        inter = sem("inter")
        post_v = sem("post_v")
        post_a = sem("post_a")
        v_to_a = sem("v_to_a")
        a_to_v = sem("a_to_v")
        v_own = sem("v_own")
        a_own = sem("a_own")
        gelu_done = sem("gelu_done")
        cm_sum = sem("cm_sum")
        cm_sq = sem("cm_sq")
        cm_add = sem("cm_add")
        cmv_out = sem("cmv_out")
        silu_r = sem("silu_r")
        osq_a = sem("osq_a")
        osq_rdy = sem("osq_rdy")
        mix_done = sem("mix_done")
        s0_split_h = sem("s0_split_h")
        s0_split = sem("s0_split")
        s0_in = [sem(f"s0_in{i}") for i in range(2)]
        s0_out = [sem(f"s0_out{i}") for i in range(2)]
        x_back = sem("x_back")
        h_done = sem("h_done")
        hsq_done = sem("hsq_done")
        hsq_add = sem("hsq_add")
        var_done = sem("var_done")
        std_done = sem("std_done")
        rstd_ok = sem("rstd_ok")
        gate_act = sem("gate_act")
        hid_f = sem("hid_f")
        hid_h = sem("hid_h")
        hid_rdy = sem("hid_rdy")
        y_scaled = sem("y_scaled")
        var_col = sem("var_col")
        std_col = sem("std_col")
        diagonals = sem("diagonals")
        factor_psum = sem("factor_psum")
        factor_copy = sem("factor_copy")
        out_v = sem("out_v")
        out_p = sem("out_p")
        stored = sem("stored")

        plan, order = mixer_plan()

        def number(piece):
            return order.index(piece) + 1

        def parts(kinds, piece):
            return sum(p[0] in kinds for p in order[:number(piece)])

        def landed(c, slot):
            return c * 8 - 8 * (slot % RAW)

        block = ctx.enter_context(nc.Block())

        @block.sync
        def _(sp):
            def load(slot, src, c, cols=CH):
                if not isinstance(c, int) or c >= 4:
                    sp.wait_ge(hi_ready, c - 3)
                    sp.wait_ge(lo_ready, c - 3)
                sp.dma_start(w_raw[:, slot % RAW, 0:cols], src).then_inc(w_landed[slot % RAW], 16)

            def load_x(i):
                sp.dma_start(trunk[:, 2 * i:2 * i + 2, :], xT[:, 2 * i:2 * i + 2, :]).then_inc(x_in[i], 16)

            sp.dma_start(vec[:], vecs).then_inc(consts_in, 16)
            load_x(0)
            sp.dma_start(al_raw, w_alr.rearrange("p k m -> p (k m)")).then_inc(alr_w_in, 16)
            load(2, w_in[0], 2)
            load_x(1)
            load(3, w_in[1], 3)
            for i in range(2, 8):
                load_x(i)
                if i in (3, 5):
                    load(4 + i // 4, w_in[2 + i // 4], 4 + i // 4)
            for dst, src in ((idn[:], ident), (triu[:], tri), (mA[:], maskA), (mS[2 * TS:], maskS), (bm[:], bmask),
                             (wa2s, wa2), (wmm, wm), (wsb[:], wsbd), (bsb, bs.partition_broadcast(P)),
                             (cbs[:], cbuf)):
                sp.dma_start(dst, src).then_inc(mid_in, 16)

            def s0_dram(t, i):
                return t[i // 2, i % 2]

            def store_s0(i):
                sp.wait_ge(post_v, parts(V_KINDS, ("s", i + 2)))
                sp.dma_start(s0_dram(gla_s, i), S0[:, i % 2, :]).then_inc(s0_out[i % 2], 16)

            def load_s0(i, again=0):
                if again and i >= 2:
                    sp.wait_ge(s0_out[i % 2], 16 * (i // 2))
                elif again or i >= 2:
                    sp.wait_ge(s0_split, again * 8 + i - 1)
                else:
                    sp.wait_ge(inter, number(("zc", 1)))
                    sp.wait_ge(post_v, parts(V_KINDS, ("zc", 1)))
                sp.dma_start(S0[:, i % 2, :], s0_dram(s0, i)).then_inc(s0_in[i % 2], 16)

            for c in range(6, C_OUT):
                if c == ZC_AT[1] + 8:
                    load_s0(0)
                    load_s0(1)
                for i in range(8):
                    if c == QS_AT[i] + 6:
                        load_s0((i + 2) % 8, (i + 2) // 8)
                    if c == S_AT[2 + i] + 7:
                        store_s0(i)
                    if c == S_AT[2 + i] + 8 and i + 2 < 8:
                        load_s0(i + 2, 1)
                if c == S_AT[-1] + 8:
                    sp.wait_ge(post_v, parts(V_KINDS, ("p", PAIRS - 1)))
                    sp.dma_start(gla_p.rearrange("h d e -> d h e"), S[:]).then_inc(stored, 16)
                    sp.wait_ge(inter, number(("s", 9)))
                    for i in range(4):
                        sp.dma_start(trunk[:, 4 * i:4 * i + 4, :], xT[:, 4 * i:4 * i + 4, :]).then_inc(x_back, 16)
                load(c, w_in[c - 2], c)
            with sp.Fori(0, KT // 2) as i:
                for s in range(4):
                    load(C_OUT + s, w_out[i * 4 + s], i * 4 + (C_OUT + s))
            sp.wait_ge(mix_done, 8)
            sp.dma_start(conv_o, cst[:]).then_inc(stored, 16)
            with sp.Fori(0, GROUPS) as gr:
                with sp.Fori(0, FG) as f:
                    for s in range(4):
                        load(C_FF + s, w_gu[gr * C_GU + f * 4 + s], gr * C_GRP + f * 4 + (C_FF + s))
                with sp.Fori(0, KT // 2) as i:
                    for s in range(4):
                        m = gr * KT + i * 2 + s // 2
                        src, cols = (w_db[m], (FG - DA) * P) if s % 2 else (w_da[m], DA * P)
                        load(C_FF + s, src, gr * C_GRP + i * 4 + (C_FF + C_GU + s), cols)
            for a in range(2):
                sp.wait_ge(out_v, 2 * a + 2)
                sp.dma_start(yT[:, 0:2, a * TH:(a + 1) * TH], trunk[:, 0:2, a * TH:(a + 1) * TH])\
                    .then_inc(stored, 16)
            for k in OUT_ORDER:
                done, n = (out_v, k + 4) if k < NV_OUT else (out_p, k + 2 - NV_OUT)
                sp.wait_ge(done, n)
                sp.dma_start(yT[:, k:k + 2, :], trunk[:, k:k + 2, :]).then_inc(stored, 16)
            sp.wait_ge(stored, 16 * (1 + 1 + 2 + len(OUT_ORDER)))
            sp.wait_ge(cmv_out, 16)
            sp.wait_ge(s0_out[0], 16 * 4)
            sp.wait_ge(s0_out[1], 16 * 4)

        @block.gpsimd
        def _(pool):
            nc.gpsimd.memset(one[:], 0.0).then_inc(zeroed, 1)
            pool.wait_ge(zeroed, 1)
            nc.gpsimd.memset(onesf[:], 1.0).then_inc(zeroed, 1)
            pool.wait_ge(zeroed, 2)
            nc.gpsimd.memset(alw[:].bitcast(F32), 0.0).then_inc(zeroed, 1)
            pool.wait_ge(zeroed, 3)
            nc.gpsimd.memset(ATs, 0.0).then_inc(zeroed, 1)
            pool.wait_ge(zeroed, 4)
            nc.gpsimd.memset(alr[2 * RANK:2 * RANK + 1, :], 1.0).then_inc(zeroed, 1)
            pool.wait_ge(zeroed, 5)
            nc.gpsimd.memset(zp[:, 0:2], 0.0).then_inc(zeroed, 1)
            pool.wait_ge(zeroed, 6)
            pool.wait_ge(mid_in, 16 * 10)
            w3 = wmm.rearrange("p (h t) -> p h t", h=4)
            nc.gpsimd.affine_select(out=w3, in_=w3, compare_op=ALU.is_ge, fill=0.0, base=0,
                                    pattern=[[0, 4], [1, P]], channel_multiplier=-1).then_inc(zeroed, 1)
            pool.wait_ge(zeroed, 7)
            nc.gpsimd.affine_select(out=wsb[:], in_=wsb[:], compare_op=ALU.is_ge, fill=0.0, base=0,
                                    pattern=[[0, 4], [1, TS]], channel_multiplier=-1).then_inc(zeroed, 1)
            pool.wait_ge(factor_copy, 1)
            pool.wait_ge(y_scaled, KT)
            for k in range(NV_OUT, KT):
                nc.gpsimd.tensor_tensor(trunk[:, k, :], trunk[:, k, :], rstd[:], ALU.mult).then_inc(out_p, 1)

        @block.scalar
        def _(act):
            own, took = Count(), Count()

            def chain(ins):
                ins.then_inc(a_own, 1)
                act.wait_ge(a_own, own.up())

            def load_tables(function):
                chain(nc.scalar.activation(one[:], one[:], function))

            def take():
                act.wait_ge(v_to_a, took.up())

            def split_hi(c, slot):
                act.wait_ge(w_landed[slot % RAW], landed(c, slot))
                if not isinstance(c, int) or c >= 6:
                    act.wait_ge(chunk_done, c - 3)
                nc.scalar.copy(w_hi[:, slot % RING, :], w_raw[:, slot % RAW, :]).then_inc(hi_ready, 1)

            act.wait_ge(zeroed, 1)
            load_tables(ACT.Sqrt)
            act.wait_ge(consts_in, 16)
            act.wait_ge(alr_w_in, 16)
            act.wait_ge(zeroed, 3)
            nc.scalar.copy(alw[:, :, 0:RANK], al_raw.rearrange("p (k m) -> p k m", k=KT)).then_inc(alr_hi, 1)
            for k in range(KT):
                act.wait_ge(x_in[k // 2], 16)
                nc.scalar.mul(op_hi[:, k, :], trunk[:, k, :], vec[:, V_G1 + k:V_G1 + k + 1]).then_inc(op_h, 1)
                if k in SPLIT_AT:
                    split_hi(SPLIT_AT[k], SPLIT_AT[k])
            def early(out, src):
                nc.scalar.copy(two(out), src).then_inc(acc_free, 1)

            act.wait_ge(alr_w, 1)
            for k in range(KT):
                if k >= 2:
                    act.wait_ge(sq_add, k - 1)
                nc.scalar.activation(tmp[:, k % 2, :], trunk[:, k, :], ACT.Square).then_inc(sq_done, 1)
                if k == HK:
                    split_hi(6, 6)
                    act.wait_ge(chunk_done, 4)
                    early(alr[0:2 * RANK, :], g23[0:2 * RANK, :, 0:TH])
                    early(qT[:, 0, :], accv(1))

            def split_s0_hi(i):
                act.wait_ge(s0_in[i % 2], 16 * (i // 2 + 1))
                if i >= 2:
                    act.wait_ge(inter, number(("qs", i - 2)))
                nc.scalar.copy(s0_hi[:, i % 2, :], S0[:, i % 2, :]).then_inc(s0_split_h, 1)

            def silu(i):
                take()
                nc.scalar.activation(tmp[:, i % 2, :], tmp[:, i % 2, :], ACT.Silu).then_inc(silu_r, 1)

            def out_squares(h):
                for e in range(2):
                    nc.scalar.activation(osq[:, e, :], mix[:, 2 * h + e, :], ACT.Square).then_inc(osq_a, 1)

            def post(kind, i):
                act.wait_ge(inter, number((kind, i)))
                last = None
                if kind == "var1":
                    last = nc.scalar.activation(two(rstd[:]), g01[:, :, 0:TH], ACT.Sqrt, bias=EPS, scale=1.0 / D)
                elif kind == "z":
                    js = range(4) if i == 0 else (4,)
                    rows = P if i == 0 else TS
                    for j in js:
                        last = nc.scalar.activation(loga[0:rows, j, :], g[j % 4][0:rows, :], ACT.Abs)
                    chain(last)
                    for j in js:
                        last = nc.scalar.activation(loga[0:rows, j, :], loga[0:rows, j, :], ACT.Exp, scale=-1.0)
                    chain(last)
                    for j in js:
                        last = nc.scalar.activation(loga[0:rows, j, :], loga[0:rows, j, :], ACT.Ln, bias=1.0)
                        if j < 3:
                            last.then_inc(a_to_v, 1)
                elif kind == "b":
                    w = 4 * (P if i < 4 else TS)
                    nc.scalar.activation(ex_p[:, 0:w], g[0][:, 0:w], ACT.Exp).then_inc(a_to_v, 1)
                    nc.scalar.activation(ex_n[:, 0:w], g[0][:, 0:w], ACT.Exp, scale=-1.0).then_inc(a_to_v, 1)
                    take()
                    last = nc.scalar.activation(ex_g[:, 0:w], ex_g[:, 0:w], ACT.Exp)
                elif kind == "mu":
                    for h in range(4):
                        take()
                        if h >= 2:
                            act.wait_ge(cm_add, h - 1)
                        last = nc.scalar.activation(tmp[:, h % 2, :], mix[:, 12 + h, :], ACT.Square)
                        if h < 3:
                            last.then_inc(cm_sq, 1)
                elif kind == "var_cm":
                    last = nc.scalar.activation(two(lnb), g23[:, :, 0:TH], ACT.Sqrt, bias=EPS, scale=1.0 / (4 * P))
                elif kind == "vvt":
                    act.wait_ge(post_v, parts(V_KINDS, ("var_cm", 0)))
                    act.dma_start(cmv, mix[:, 12:16, TP:T]).then_inc(cmv_out, 16)
                    nc.scalar.copy(vvt[:, 2, :], g[2])
                    last = nc.scalar.copy(vvt[:, 3, :], g[3])
                elif kind == "p":
                    last = nc.scalar.copy(mix[:, 0:8, P * i:P * (i + 1)],
                                          g01[:].rearrange("p a (s t) -> p (a s) t", s=4))
                elif kind == "s":
                    if i == 1:
                        nc.scalar.copy(vs4[0:TS, :], vs)
                        nc.scalar.copy(vs4[2 * TS:3 * TS, :], vs).then_inc(a_to_v, 1)
                        last = nc.scalar.copy(mix[:, 0:8, TP:T], g[0][:, 0:8 * TS].rearrange("p (s t) -> p s t", s=8))
                elif kind == "on":
                    last = nc.scalar.activation(two(orstd), g01[:, :, 0:TH], ACT.Sqrt, bias=EPS, scale=1.0 / DV)
                if last is None:
                    last = act.nop()
                last.then_inc(post_a, 1)
                if kind == "on" and i < 3:
                    out_squares(i + 1)

            def evac(t):
                if T_CV <= t < T_V:
                    j = t - T_CV
                    take()
                    m = mix[:, 12 + j if t < T_CU else 4 + j, :]
                    nc.scalar.activation(m, m, ACT.Gelu).then_inc(gelu_done, 1)
                elif t >= T_R:
                    silu(t - T_R)

            def op_hi_tile(k):
                act.wait_ge(mix_done, 8 if k < 8 else k + 1)
                nc.scalar.copy(op_hi[:, k, :], mix[:, MIX_ORDER[k], :]).then_inc(op_h, 1)

            for c in range(3, C_OUT):
                act.wait_ge(chunk_done, c + 1)
                if c == C_OUT - 1:
                    evac(c // 2)
                    for k in range(HK, KT):
                        op_hi_tile(k)
                    split_hi(c + 4, c + 4)
                    continue
                if c == 5:
                    early(qT[:, 1, :], accv(2))
                if c % 2 and c > 5:
                    evac(c // 2)
                for kind, i in plan.get(c, ()):
                    if kind in A_KINDS:
                        post(kind, i)
                if c == OSQ_AT:
                    act.wait_ge(post_v, parts(V_KINDS, ("s", 9)))
                    act.wait_ge(post_v, parts(V_KINDS, ("p", PAIRS - 1)))
                    out_squares(0)
                split_hi(c + 4, c + 4)
                if c + 2 in QS_AT:
                    split_s0_hi(QS_AT.index(c + 2))
                if c == C_OUT - 2:
                    for k in range(HK):
                        op_hi_tile(k)

            def gfs(i, odd):
                if isinstance(i, int):
                    return vec[:, V_GF + 2 * i + odd:V_GF + 2 * i + odd + 1]
                return vec[:, bass.ds(i * 2 + (V_GF + odd), 1)]

            def square_h(m, par, base):
                act.wait_ge(hsq_add, m + (base[1] - 1))
                act.wait_ge(h_done, m + (base[0] + 1))
                nc.scalar.activation(tmp[:, par, :], trunk[:, m, :], ACT.Square).then_inc(hsq_done, 1)

            def sqrt_var(n):
                act.wait_ge(var_done, n)
                nc.scalar.activation(two(rstd[:]), g01[:, :, 0:TH], ACT.Sqrt, bias=EPS, scale=1.0 / D)\
                    .then_inc(std_done, 1)

            def op_hi_h(ks):
                for k in ks:
                    act.wait_ge(h_done, k + 1)
                    nc.scalar.mul(op_hi[:, k, :], trunk[:, k, :], vec[:, V_G2 + k:V_G2 + k + 1]).then_inc(op_h, 1)

            def out_tiles(i, tail):
                for s in range(4):
                    c = i * 4 + (C_OUT + s)
                    act.wait_ge(chunk_done, c + 1)
                    if s % 2:
                        square_h(i * 2 + s // 2, s // 2, NORM_2)
                    if tail and s == 3:
                        op_hi_h(range(HK, KT))
                    split_hi(c + 4, C_OUT + s + 4)
                    if tail and s == 2:
                        op_hi_h(range(HK))

            with act.Fori(0, KT // 2 - 1) as i:
                out_tiles(i, False)
            out_tiles(KT // 2 - 1, True)
            sqrt_var(1)
            load_tables(ACT.Silu)

            def group(gr, last):
                with act.Fori(0, FG) as f:
                    for s in range(4):
                        c = gr * C_GRP + f * 4 + (C_FF + s)
                        act.wait_ge(chunk_done, c + 1)
                        if s == 1:
                            act.wait_ge(acc_free, gr * (C_GRP // 2) + f * 2 + (C_FF // 2 + 1))
                            nc.scalar.activation(tmp[:, 1, :], tmp[:, 1, :], ACT.Silu).then_inc(gate_act, 1)
                        if s == 3:
                            act.wait_ge(hid_f, gr * FG + f + 1)
                            nc.scalar.copy(hid_hi[:, f, :], tmp[:, 0, :]).then_inc(hid_h, 1)
                        split_hi(c + 4, C_FF + s + 4)

                def down(i, tail):
                    for s in range(4):
                        c = gr * C_GRP + i * 4 + (C_FF + C_GU + s)
                        act.wait_ge(chunk_done, c + 1)
                        if last and s % 2:
                            m = i * 2 + s // 2
                            square_h(m, s // 2, NORM_F)
                            nc.scalar.mul(trunk[:, m, :], trunk[:, m, :], gfs(i, s // 2)).then_inc(y_scaled, 1)
                        if not tail:
                            split_hi(c + 4, C_FF + s + 4)

                if last:
                    load_tables(ACT.Sqrt)
                with act.Fori(0, KT // 2 - (1 if last else 0)) as i:
                    down(i, False)
                if last:
                    down(KT // 2 - 1, True)

            with act.Fori(0, GROUPS - 1) as gr:
                group(gr, False)
            group(GROUPS - 1, True)
            act.wait_ge(var_col, 1)
            nc.scalar.activation(colf, colf, ACT.Sqrt, bias=EPS, scale=1.0 / D).then_inc(std_col, 1)
            act.wait_ge(factor_psum, 4)
            nc.scalar.copy(two(rstd[:]), accv(0)).then_inc(factor_copy, 1)

        @block.tensor
        def _(pe):
            def products(t, slot, j, k, start, stop, rhs_hi, rhs_lo):
                w_h = w_hi[:, slot % RING, j * P:(j + 1) * P]
                w_l = w_lo[:, slot % RING, j * P:(j + 1) * P]
                for n, (w, x) in enumerate(((w_h, rhs_hi), (w_h, rhs_lo), (w_l, rhs_hi))):
                    for a in range(2):
                        last = nc.tensor.matmul(acc[t % 2][:, a, 0:TH], w, x[:, k, a * TH:(a + 1) * TH],
                                                start=start and n == 0, stop=stop and n == 2)
                return last

            def chunk(c, slot, t, par, ks, start, stop, rhs_hi=op_hi, rhs_lo=op_lo, ready=None):
                pe.wait_ge(hi_ready, c - 1)
                pe.wait_ge(lo_ready, c - 1)
                if start and not isinstance(t, int) or start and t > 2:
                    pe.wait_ge(acc_free, t - 1)
                for j, k in enumerate(ks):
                    if ready is not None:
                        ready(k)
                    last = products(par, slot, j, k, start and j == 0, stop and j == len(ks) - 1, rhs_hi, rhs_lo)
                last.then_inc(chunk_done, 1)

            pe.wait_ge(zeroed, 2)
            for _ in range(WARM):
                nc.tensor.matmul(g01[:, 0, 0:P], onesf[:], onesf[:], start=True, stop=True)

            pe.wait_ge(alr_w, 1)
            for k in range(KT):
                pe.wait_ge(op_rdy, k + 1)
                for n, x in enumerate((op_hi, op_lo)):
                    for a in range(2):
                        mm = nc.tensor.matmul(g23[:, a, 0:TH], alw[:, k, :], x[:, k, a * TH:(a + 1) * TH],
                                              start=(k == 0 and n == 0), stop=(k == KT - 1 and n == 1))
                        if k == KT - 1 and n == 1:
                            mm.then_inc(chunk_done, 1)
                if k % HK == 0:
                    pe.wait_ge(hi_ready, 1 + k // HK)
                    pe.wait_ge(lo_ready, 1 + k // HK)
                mm = products(1, 2 + k // HK, k % HK, k, k == 0, k == KT - 1, op_hi, op_lo)
                if k % HK == HK - 1:
                    mm.then_inc(chunk_done, 1)

            def ones_product(out2, buf):
                for a in range(2):
                    last = nc.tensor.matmul(out2[:, a, 0:TH], onesf[:], buf[:, a * TH:(a + 1) * TH],
                                            start=True, stop=True)
                return last

            def kd_transposes(i):
                w = P if i < 4 else TS
                for h in range(HEADS):
                    last = nc.tensor.transpose(g[1][0:w, h * P:(h + 1) * P], ex_g[:, h * w:(h + 1) * w], idn[:])
                return last

            def scores(i):
                for h in range(HEADS):
                    for r in (0, CHUNK):
                        tok = slice(i * P + r, i * P + r + CHUNK)
                        nc.tensor.matmul(g[2][r:r + CHUNK, h * P + r:h * P + r + CHUNK], kT[:, h, tok],
                                         qT[:, h, tok], start=True, stop=True)
                    nc.tensor.matmul(g[2][0:CHUNK, h * P + CHUNK:(h + 1) * P], ex_p[:, h * P:h * P + CHUNK],
                                     qT[:, h, i * P + CHUNK:(i + 1) * P], start=True, stop=True)

            def piece(kind, i):
                n = number((kind, i))
                before = order[:n - 1]
                if kind == "qs" and before[-1][0] == "vt":
                    before = before[:-1]
                if any(p[0] in V_KINDS for p in before):
                    pe.wait_ge(post_v, sum(p[0] in V_KINDS for p in before))
                if any(p[0] in A_KINDS for p in before):
                    pe.wait_ge(post_a, sum(p[0] in A_KINDS for p in before))
                if kind == "var1":
                    pe.wait_ge(zeroed, 6)
                    pe.wait_ge(sq_add, KT)
                    last = ones_product(g01, rstd[:])
                elif kind == "z":
                    pe.wait_ge(mid_in, 16 * 10)
                    for j in (range(4) if i == 0 else (4,)):
                        rows = P if j < 4 else TS
                        last = nc.tensor.matmul(g[j % 4][0:rows, :], alr[:, j * P:j * P + rows], wa2s,
                                                start=True, stop=True)
                elif kind == "b":
                    if i == 0:
                        pe.wait_ge(acc_free, T_CV)
                    if i >= 1:
                        kd_transposes(i - 1)
                        scores(i - 1)
                    w, tr = (P, triu[:, 0:P]) if i < 4 else (TS, triu[0:TS, P:P + TS])
                    for h in range(HEADS):
                        last = nc.tensor.matmul(g[0][:, h * w:(h + 1) * w], loga[0:w, i, h * P:(h + 1) * P], tr,
                                                start=True, stop=True)
                elif kind == "kdt":
                    last = kd_transposes(4)
                elif kind == "mu":
                    pe.wait_ge(cm_sum, 3)
                    last = ones_product(g23, lnb)
                elif kind == "var_cm":
                    last = ones_product(g23, lnb)
                elif kind == "vvt":
                    for j in range(4):
                        for h in range(4):
                            last = nc.tensor.transpose(g[j][:, h * P:(h + 1) * P],
                                                       mix[:, 12 + h, j * P:(j + 1) * P], idn[:])
                elif kind == "zc":
                    if i == 0:
                        pe.wait_ge(zeroed, 8)
                        for h in range(4):
                            nc.tensor.transpose(g[0][0:TS, h * P:(h + 1) * P], mix[:, 12 + h, TP:T], idn[:])
                    for h in (range(3) if i == 0 else (3,)):
                        for j in range(4):
                            last = nc.tensor.matmul(g[(h + 1) % 4][:, j * P:(j + 1) * P], vvt[:, j, h * P:(h + 1) * P],
                                                    wmm[:, h * P:(h + 1) * P], start=True, stop=True)
                    if i == 1:
                        for h in range(4):
                            last = nc.tensor.matmul(g[1][:, h * TS:(h + 1) * TS], vvts[:, h * P:(h + 1) * P],
                                                    wsb[:, h, :], start=True, stop=True)
                elif kind == "vt":
                    pe.wait_ge(acc_free, T_V + i + 1)
                    for j in range(4):
                        nc.tensor.transpose(g[2][:, j * P:(j + 1) * P], tmp[:, i % 2, j * P:(j + 1) * P], idn[:])
                    last = nc.tensor.transpose(g[3][0:TS, 0:P], tmp[:, i % 2, TP:T], idn[:])
                elif kind == "p":
                    tok = slice(P * i, P * (i + 1))
                    for h in range(HEADS):
                        for e in range(2):
                            out = g[h // 2][:, (2 * (h % 2) + e) * P:(2 * (h % 2) + e + 1) * P]
                            nc.tensor.matmul(out, v[:, i, h * DV + e * P:h * DV + (e + 1) * P], AT[:, h, tok],
                                             start=True, stop=(i == 0))
                            if i > 0:
                                nc.tensor.matmul(out, S[:, h, e * P:(e + 1) * P], qT[:, h, tok],
                                                 start=False, stop=True)
                    for h in range(HEADS):
                        last = nc.tensor.matmul(g[2 + h // 2][:, (h % 2) * DV:(h % 2 + 1) * DV],
                                                kd[:, i, h * P:(h + 1) * P], v[:, i, h * DV:(h + 1) * DV],
                                                start=True, stop=True)
                elif kind == "qs":
                    h, half = i // 2, i % 2
                    pe.wait_ge(s0_split, i + 1)
                    for b in range(4):
                        for n, x in enumerate((s0_hi, s0_lo)):
                            last = nc.tensor.matmul(g[h // 2][:, (h % 2) * DV:(h % 2 + 1) * DV],
                                                    qm[:, (4 * half + b) * P:(4 * half + b + 1) * P],
                                                    x[:, i % 2, b * DV:(b + 1) * DV],
                                                    start=(half + b + n == 0), stop=(half + b + n == 5))
                elif kind == "s":
                    for h in range(HEADS) if i < 2 else ():
                        if i == 0:
                            last = nc.tensor.matmul(g[0][2 * TS:3 * TS, h * TS:(h + 1) * TS], kT[:, h, TP:T],
                                                    qT[:, h, TP:T], start=True, stop=True)
                        else:
                            for e in range(2):
                                out = g[0][:, (2 * h + e) * TS:(2 * h + e + 1) * TS]
                                cols = slice(h * DV + e * P, h * DV + (e + 1) * P)
                                last = nc.tensor.matmul(out, ov[:, cols], ovm[:, h * TS:(h + 1) * TS],
                                                        start=True, stop=True)
                    if i >= 2:
                        n = i - 2
                        h, half = n // 2, n % 2
                        for b in range(4):
                            last = nc.tensor.matmul(g[2 + b // 2][:, (b % 2) * DV:(b % 2 + 1) * DV], kdm[:, b, :],
                                                    vs4[:, h * DV:(h + 1) * DV], start=True, stop=True)
                elif kind == "on":
                    pe.wait_ge(osq_rdy, i + 1)
                    last = ones_product(g01, osq[:, 0, :])
                last.then_inc(inter, 1)

            for c in range(3, C_OUT):
                if c > 3:
                    t, half = c // 2, c % 2
                    chunk(c, c, t, t, range(HK * half, HK * (half + 1)), half == 0, half == 1)
                for kind, i in plan.get(c, ()):
                    piece(kind, i)

            def op_ready(base):
                def ready(k):
                    if k % 2 == 0:
                        pe.wait_ge(op_rdy, base + k + 2)
                return ready

            with pe.Fori(0, KT // 2) as i:
                for s in range(4):
                    half = s % 2
                    chunk(i * 4 + (C_OUT + s), C_OUT + s, i * 2 + (N_IN + s // 2), N_IN + s // 2,
                          range(HK * half, HK * (half + 1)), half == 0, half == 1,
                          ready=op_ready(KT) if s < 2 else None)

            def sum_squares(n_add):
                pe.wait_ge(hsq_add, n_add)
                ones_product(g01, rstd[:]).then_inc(var_done, 1)

            def gate_up(gr, f, first=False):
                for s in range(4):
                    half = s % 2
                    chunk(gr * C_GRP + f * 4 + (C_FF + s), C_FF + s,
                          gr * (C_GRP // 2) + f * 2 + (C_FF // 2 + s // 2), C_FF // 2 + s // 2,
                          range(HK * half, HK * (half + 1)), half == 0, half == 1,
                          ready=op_ready(2 * KT) if first and s < 2 else None)
                    if first and s == 0:
                        sum_squares(2 + KT)

            def down(gr):
                def hid_ready(k):
                    if k == 0:
                        pe.wait_ge(hid_rdy, gr * FG + (FG - 1))
                    if k == FG - 1:
                        pe.wait_ge(hid_rdy, gr * FG + FG)

                with pe.Fori(0, KT // 2) as i:
                    for s in range(4):
                        half = s % 2
                        chunk(gr * C_GRP + i * 4 + (C_FF + C_GU + s), C_FF + s,
                              gr * (C_GRP // 2) + i * 2 + ((C_FF + C_GU) // 2 + s // 2), (C_FF + C_GU) // 2 + s // 2,
                              range(DA * half, DA if half == 0 else FG), half == 0, half == 1,
                              hid_hi, hid_lo, ready=hid_ready)

            gate_up(0, 0, first=True)
            with pe.Fori(1, FG) as f:
                gate_up(0, f)
            down(0)
            with pe.Fori(1, GROUPS) as gr:
                with pe.Fori(0, FG) as f:
                    gate_up(gr, f)
                down(gr)
            pe.wait_ge(hsq_add, NORM_F[1] + KT - 1)
            for n, buf in enumerate((rstd[:], tmp[:, (KT - 1) % 2, :])):
                if n == 1:
                    pe.wait_ge(hsq_done, 2 * KT)
                for j, (at, _, _) in enumerate(BLOCKS):
                    last = nc.tensor.matmul(g01[:, n, j:j + 1], buf[:, at:at + P], onesf[:, 0:1], start=True, stop=True)
            last.then_inc(var_done, 1)
            for out in (g23, acc[0]):
                for j, (_, skip, w) in enumerate(BLOCKS):
                    pe.wait_ge(diagonals, j // 3 + 1)
                    at = BLOCKS[j][0] + skip
                    last = nc.tensor.matmul(out[:, at // TH, at % TH:at % TH + w], onesf[:],
                                            diag[:, j * P + skip:j * P + skip + w], start=True, stop=True)
                    if j % 3 == 2:
                        last.then_inc(factor_psum, 1)

        @block.vector
        def _(dve):
            own, took = Count(), Count()

            def chain(ins):
                ins.then_inc(v_own, 1)
                dve.wait_ge(v_own, own.up())

            def take():
                dve.wait_ge(a_to_v, took.up())

            def f32(ap):
                return ap.bitcast(F32)

            def split_lo(c, slot):
                dve.wait_ge(hi_ready, c - 1)
                nc.vector.tensor_tensor(w_lo[:, slot % RING, :], w_raw[:, slot % RAW, :],
                                        f32(w_hi[:, slot % RING, :]), ALU.subtract).then_inc(lo_ready, 1)

            def op_lo_scaled(k, n, gcol):
                dve.wait_ge(op_h, n)
                nc.vector.scalar_tensor_tensor(out=op_lo[:, k, :], in0=trunk[:, k, :], scalar=vec[:, gcol:gcol + 1],
                                               in1=f32(op_hi[:, k, :]), op0=ALU.mult, op1=ALU.subtract)\
                    .then_inc(op_rdy, 1)

            dve.wait_ge(alr_hi, 1)
            nc.vector.tensor_tensor(alw[:, :, RANK:2 * RANK], al_raw.rearrange("p (k m) -> p k m", k=KT),
                                    f32(alw[:, :, 0:RANK]), ALU.subtract).then_inc(alr_w, 1)
            for k in range(KT):
                op_lo_scaled(k, k + 1, V_G1 + k)
                if k in SPLIT_AT:
                    split_lo(SPLIT_AT[k], SPLIT_AT[k])
            for k in range(KT):
                dve.wait_ge(sq_done, k + 1)
                if k == 0:
                    nc.vector.tensor_copy(rstd[:], tmp[:, 0, :]).then_inc(sq_add, 1)
                else:
                    dve.wait_ge(sq_add, k)
                    nc.vector.tensor_tensor(rstd[:], rstd[:], tmp[:, k % 2, :], ALU.add).then_inc(sq_add, 1)
                if k == HK:
                    split_lo(6, 6)

            def normalised(out, src, rows=P):
                nc.vector.tensor_tensor(out, src[0:rows, :, 0:TH], two(rstd[0:rows, :]), ALU.mult)\
                    .then_inc(acc_free, 1)

            def kd_out(i):
                if i < 4:
                    return nc.vector.tensor_copy(kd[:, i, :], g[1])
                nc.vector.tensor_copy(kd4[0:TS, :], g[1][0:TS, :])
                chain(nc.vector.tensor_copy(kd4[TS:2 * TS, :], g[1][0:TS, :]))
                for q in (2, 3):
                    last = nc.vector.tensor_tensor(kd4[q * TS:(q + 1) * TS, :], g[1][0:TS, :], f32(kd4[0:TS, :]),
                                                   ALU.subtract)
                return last

            def decay(n):
                return egp[:, n, :].unsqueeze(2).to_broadcast([P, HEADS, CHUNK])

            def scores_out(i):
                tok = slice(i * P, (i + 1) * P)
                chain(nc.vector.memset(AT[:, :, tok], 0.0))
                sc = g[2].rearrange("p (h t) -> p h t", h=HEADS)
                m3 = mA[:].rearrange("p (h t) -> p h t", h=HEADS)
                for r in (0, CHUNK):
                    nc.vector.copy_predicated(AT[r:r + CHUNK, :, i * P + r:i * P + r + CHUNK], m3[r:r + CHUNK],
                                              sc[r:r + CHUNK, :, r:r + CHUNK])
                nc.vector.tensor_copy(AT[0:CHUNK, :, i * P + CHUNK:(i + 1) * P], sc[0:CHUNK, :, CHUNK:])
                q2 = qT[:, :, i * P + CHUNK:(i + 1) * P]
                nc.vector.tensor_tensor(q2, q2, decay(2 * i), ALU.mult)

            def query_blocks(h):
                q = qT[:, h, TP:T].rearrange("p (b t) -> p b t", b=DB)
                hi, lo = (qm[:, n:n + DB * QB].rearrange("p (b c) -> p b c", b=DB)[:, :, 0:DS] for n in (0, TS))
                chain(nc.vector.tensor_copy(hi, q))
                return nc.vector.tensor_tensor(lo, q, f32(hi), ALU.subtract)

            def split_s0_lo(i):
                if i == 0:
                    for r in (0, TS):
                        nc.vector.tensor_copy(ovm[r:r + TS, :].rearrange("s (h t) -> s h t", h=HEADS),
                                              idn[r:r + TS, r:r + TS].unsqueeze(1).to_broadcast([TS, HEADS, TS]))
                    chain(nc.vector.memset(f32(qm[:]), 0.0))
                    query_blocks(0)
                dve.wait_ge(s0_split_h, i + 1)
                nc.vector.tensor_tensor(s0_lo[:, i % 2, :], S0[:, i % 2, :], f32(s0_hi[:, i % 2, :]), ALU.subtract)\
                    .then_inc(s0_split, 1)

            def mask_kd(n):
                h, half = n // 2, n % 2
                return nc.vector.tensor_tensor(kdm[:],
                                               f32(kd4[:, h * P:(h + 1) * P]).unsqueeze(1).to_broadcast([P, 4, P]),
                                               bm[:, 4 * half:4 * half + 4].unsqueeze(2).to_broadcast([P, 4, P]),
                                               ALU.mult)

            def out_square_sum(h):
                dve.wait_ge(osq_a, 2 * h + 2)
                nc.vector.tensor_tensor(osq[:, 0, :], osq[:, 0, :], osq[:, 1, :], ALU.add).then_inc(osq_rdy, 1)

            def post(kind, i):
                dve.wait_ge(inter, number((kind, i)))
                last = None
                if kind == "var1":
                    dve.wait_ge(post_a, parts(A_KINDS, (kind, i)))
                    chain(nc.vector.reciprocal(rstd[:], rstd[:]))
                    dve.wait_ge(acc_free, 3)
                    nc.vector.tensor_tensor(alr[0:2 * RANK, :], alr[0:2 * RANK, :], rstd[0:2 * RANK, :], ALU.mult)
                    for h in range(2):
                        last = nc.vector.tensor_tensor(qT[:, h, :], qT[:, h, :], rstd[:], ALU.mult)
                elif kind == "z":
                    for j in (range(4) if i == 0 else (4,)):
                        rows = P if j < 4 else TS
                        if j < 3:
                            take()
                        else:
                            dve.wait_ge(post_a, parts(A_KINDS, (kind, i)))
                        last = nc.vector.scalar_tensor_tensor(out=loga[0:rows, j, :], in0=g[j % 4][0:rows, :],
                                                              scalar=0.0, in1=loga[0:rows, j, :],
                                                              op0=ALU.min, op1=ALU.subtract)
                elif kind == "b":
                    w = P if i < 4 else TS
                    n, lc = (2, CHUNK) if i < 4 else (DB, DS)
                    tok = slice(i * P, i * P + w)
                    if i >= 1:
                        kd_out(i - 1)
                        scores_out(i - 1)
                    take()
                    take()
                    chain(nc.vector.tensor_copy(ex_g[:, 0:4 * w], g[0][:, 0:4 * w]))
                    b4 = g[0][:, 0:4 * w].rearrange("p (a l) -> p a l", l=lc)
                    x4 = ex_g[:, 0:4 * w].rearrange("p (a l) -> p a l", l=lc)
                    nc.vector.tensor_tensor(x4, b4[:, :, lc - 1:lc].to_broadcast([P, HEADS * n, lc]), x4,
                                            ALU.subtract).then_inc(v_to_a, 1)
                    ends = ex_p[:, 0:4 * w].rearrange("p (h n l) -> p h n l", h=HEADS, n=n)[:, :, :, lc - 1]
                    dst = egp[:, 2 * i:2 * i + 2, :].rearrange("p n h -> p h n") if i < 4 else egs[:]
                    nc.vector.tensor_copy(dst, ends)

                    def heads(buf):
                        return buf[:, 0:4 * w].rearrange("p (h t) -> p h t", h=HEADS)

                    chain(nc.vector.scalar_tensor_tensor(out=qT[:, :, tok], in0=qT[:, :, tok], scalar=DK ** -0.5,
                                                         in1=heads(ex_p), op0=ALU.mult, op1=ALU.mult))
                    dve.wait_ge(post_a, parts(A_KINDS, (kind, i)))
                    if i < 4:
                        eg, first = heads(ex_g), heads(ex_p)[:, :, 0:CHUNK]
                        chain(nc.vector.tensor_tensor(first, kT[:, :, i * P:i * P + CHUNK], eg[:, :, 0:CHUNK],
                                                      ALU.mult))
                        nc.vector.tensor_tensor(eg[:, :, 0:CHUNK], first, decay(2 * i + 1), ALU.mult)
                        chain(nc.vector.tensor_tensor(eg[:, :, CHUNK:], kT[:, :, i * P + CHUNK:(i + 1) * P],
                                                      eg[:, :, CHUNK:], ALU.mult))
                    else:
                        nc.vector.tensor_tensor(heads(ex_g), kT[:, :, tok], heads(ex_g), ALU.mult)
                    last = nc.vector.tensor_tensor(kT[:, :, tok], kT[:, :, tok], heads(ex_n), ALU.mult)
                elif kind == "kdt":
                    chain(kd_out(4))
                    nc.vector.tensor_tensor(egp[:, ::2, :], egp[:, ::2, :], egp[:, 1::2, :], ALU.mult)
                    last = mask_kd(0)
                elif kind == "mu":
                    for h in range(4):
                        nc.vector.scalar_tensor_tensor(out=two(mix[:, 12 + h, :]), in0=g23[:, :, 0:TH],
                                                       scalar=-1.0 / (4 * P), in1=two(mix[:, 12 + h, :]),
                                                       op0=ALU.mult, op1=ALU.add).then_inc(v_to_a, 1)
                    for h in range(4):
                        if h < 3:
                            dve.wait_ge(cm_sq, h + 1)
                        else:
                            dve.wait_ge(post_a, parts(A_KINDS, (kind, i)))
                        if h == 0:
                            last = nc.vector.tensor_copy(lnb, tmp[:, 0, :])
                        else:
                            dve.wait_ge(cm_add, h)
                            last = nc.vector.tensor_tensor(lnb, lnb, tmp[:, h % 2, :], ALU.add)
                        if h < 3:
                            last.then_inc(cm_add, 1)
                elif kind == "var_cm":
                    dve.wait_ge(post_a, parts(A_KINDS, (kind, i)))
                    chain(nc.vector.reciprocal(lnb, lnb))
                    for h in range(4):
                        last = nc.vector.scalar_tensor_tensor(out=mix[:, 12 + h, :], in0=mix[:, 12 + h, :],
                                                              scalar=vec[:, V_LG + h:V_LG + h + 1], in1=lnb,
                                                              op0=ALU.mult, op1=ALU.mult)
                    chain(last)
                    for h in range(4):
                        last = nc.vector.tensor_scalar(mix[:, 12 + h, :], mix[:, 12 + h, :],
                                                       vec[:, V_LB + h:V_LB + h + 1], None, ALU.add)
                elif kind == "vvt":
                    nc.vector.tensor_copy(vvt[:, 0, :], g[0])
                    last = nc.vector.tensor_copy(vvt[:, 1, :], g[1])
                elif kind == "zc":
                    if i == 0:
                        nc.vector.tensor_copy(vvts[:], g[0][0:TS, :])
                    hs = range(3) if i == 0 else (3,)
                    for h in hs:
                        last = nc.vector.tensor_tensor(
                            mix[:, 12 + h, 0:TP].rearrange("p (j t) -> p j t", j=4),
                            g[(h + 1) % 4].rearrange("p (j t) -> p j t", j=4),
                            bsb[:, h * P:(h + 1) * P].unsqueeze(1).to_broadcast([P, 4, P]), ALU.add)
                    if i == 1:
                        dve.wait_ge(cmv_out, 16)
                        for h in range(4):
                            last = nc.vector.tensor_tensor(
                                mix[:, 12 + h, TP:T].rearrange("p (b t) -> p b t", b=DB),
                                g[1][:, h * TS:(h + 1) * TS].rearrange("p (b t) -> p b t", b=DB),
                                bsb[:, h * P:h * P + DS].unsqueeze(1).to_broadcast([P, DB, DS]), ALU.add)
                    if i == 1:
                        chain(last)
                        dve.wait_ge(gelu_done, 8)
                        for h in range(4):
                            last = nc.vector.tensor_tensor(mix[:, 12 + h, :], mix[:, 12 + h, :], mix[:, 8 + h, :],
                                                           ALU.mult)
                            last.then_inc(mix_done, 1)
                        dve.wait_ge(mix_done, 4)
                        last = None
                elif kind == "vt":
                    nc.vector.tensor_copy(v[:, 0:4, i * P:(i + 1) * P], g[2].rearrange("p (j e) -> p j e", j=4))
                    last = nc.vector.tensor_copy(vs[:, i * P:(i + 1) * P], g[3][0:TS, 0:P])
                elif kind == "p":
                    for h in range(HEADS):
                        ds = g[2 + h // 2][:, (h % 2) * DV:(h % 2 + 1) * DV]
                        if i == 0:
                            last = nc.vector.tensor_copy(S[:, h, :], ds)
                        else:
                            last = nc.vector.scalar_tensor_tensor(out=S[:, h, :], in0=S[:, h, :],
                                                                  scalar=egp[:, 2 * i, h:h + 1], in1=ds,
                                                                  op0=ALU.mult, op1=ALU.add)
                elif kind == "qs":
                    if i % 2 and i < 7:
                        last = query_blocks(i // 2 + 1)
                    if i == 7:
                        last = nc.vector.tensor_copy(o_tok.rearrange("t (a e) -> t a e", a=2), g01[0:2 * TS])
                elif kind == "s":
                    if i == 0:
                        last = nc.vector.copy_predicated(ATs, mS[2 * TS:], g[0][2 * TS:3 * TS, 0:HEADS * TS])
                    elif i == 1:
                        take()
                        for q in (1, 3):
                            last = nc.vector.tensor_tensor(vs4[q * TS:(q + 1) * TS, :], vs, f32(vs4[2 * TS:3 * TS, :]),
                                                           ALU.subtract)
                    else:
                        n = i - 2
                        h, half = n // 2, n % 2
                        dve.wait_ge(s0_in[n % 2], 16 * (4 + n // 2 + 1))
                        if n + 1 < 8:
                            mask_kd(n + 1)
                        for b in range(4):
                            last = nc.vector.scalar_tensor_tensor(
                                out=S0[:, n % 2, b * DV:(b + 1) * DV], in0=S0[:, n % 2, b * DV:(b + 1) * DV],
                                scalar=egs[:, h, 4 * half + b:4 * half + b + 1],
                                in1=g[2 + b // 2][:, (b % 2) * DV:(b % 2 + 1) * DV], op0=ALU.mult, op1=ALU.add)
                elif kind == "on":
                    dve.wait_ge(post_a, parts(A_KINDS, (kind, i)))
                    chain(nc.vector.reciprocal(orstd, orstd))
                    if i < 3:
                        out_square_sum(i + 1)
                    for e in range(2):
                        m = 2 * i + e
                        last = nc.vector.scalar_tensor_tensor(out=mix[:, m, :], in0=mix[:, m, :],
                                                              scalar=vec[:, V_GLA + m:V_GLA + m + 1], in1=orstd,
                                                              op0=ALU.mult, op1=ALU.mult)
                if last is None:
                    last = dve.nop()
                last.then_inc(post_v, 1)

            zpp = zp[:, 0:2 + TP]
            zps = zp[:, 2 + TP:].rearrange("p (b t) -> p b t", b=DB)

            def conv_tile(i):
                nc.vector.tensor_tensor(zpp[:, 2:], tmp[:, 0, 0:TP], tmp[:, 1, 0:TP], ALU.mult)
                nc.vector.tensor_tensor(zps[:, :, 2:], tmp[:, 0, TP:T].rearrange("p (b t) -> p b t", b=DB),
                                        tmp[:, 1, TP:T].rearrange("p (b t) -> p b t", b=DB), ALU.mult)
                chain(nc.vector.tensor_copy(zps[:, :, 0:2], cbs[:, i, :].rearrange("p (b t) -> p b t", b=DB)))
                mp = mix[:, 8 + i, 0:TP]
                ms = mix[:, 8 + i, TP:T].rearrange("p (b t) -> p b t", b=DB)
                for z, m, n in ((zpp, mp, TP), (zps, ms, DS)):
                    def tap(j):
                        return z[:, j:j + n] if n == TP else z[:, :, j:j + n]
                    for j in range(3):
                        w = vec[:, V_CW + 4 * j + i:V_CW + 4 * j + i + 1]
                        if j == 0:
                            chain(nc.vector.tensor_scalar(m, tap(0), w, vec[:, V_CB + i:V_CB + i + 1],
                                                          ALU.mult, ALU.add))
                        else:
                            chain(nc.vector.scalar_tensor_tensor(out=m, in0=tap(j), scalar=w, in1=m,
                                                                 op0=ALU.mult, op1=ALU.add))
                nc.vector.tensor_copy(cst[:, i, 0:2], zpp[:, TP:TP + 2])
                nc.vector.tensor_copy(cst[:, i, 2:].rearrange("p (b t) -> p b t", b=DB), zps[:, :, DS:DS + 2])

            def evac(t):
                if t < T_CV:
                    normalised(two((qT if t < T_K else kT)[:, (t - T_Q) % 4, :]), acc[t % 2])
                elif t < T_V:
                    j = t - T_CV
                    m = mix[:, 12 + j if t < T_CU else 4 + j, :]
                    normalised(two(m), acc[t % 2])
                    dve.wait_ge(acc_free, t + 1)
                    dve.nop().then_inc(v_to_a, 1)
                    if 2 <= j <= 4:
                        dve.wait_ge(gelu_done, j)
                        if j > 2:
                            dve.wait_ge(cm_sum, j - 2)
                        nc.vector.tensor_tensor(lnb, mix[:, 12, :] if j == 2 else lnb, mix[:, 11 + j, :], ALU.add)\
                            .then_inc(cm_sum, 1)
                elif t < T_CONV:
                    normalised(two(tmp[:, (t - T_V) % 2, :]), acc[t % 2])
                elif t < T_R:
                    i, part = divmod(t - T_CONV, 3)
                    if part == 0 and i >= 1:
                        dve.wait_ge(mix_done, 4 + i)
                    normalised(two(tmp[:, 1 if part == 1 else 0, :]), acc[t % 2])
                    if part >= 1:
                        dve.wait_ge(acc_free, t + 1)
                    if part == 1:
                        conv_tile(i)
                    if part == 2:
                        nc.vector.tensor_tensor(mix[:, 8 + i, :], mix[:, 8 + i, :], tmp[:, 0, :], ALU.mult)\
                            .then_inc(mix_done, 1)
                else:
                    i = t - T_R
                    normalised(two(tmp[:, i % 2, :]), acc[t % 2])
                    dve.wait_ge(acc_free, t + 1)
                    dve.nop().then_inc(v_to_a, 1)
                    dve.wait_ge(silu_r, i + 1)
                    nc.vector.tensor_tensor(mix[:, i, :], mix[:, i, :], tmp[:, i % 2, :], ALU.mult)\
                        .then_inc(mix_done, 1)

            def op_lo_tile(k):
                dve.wait_ge(op_h, KT + k + 1)
                nc.vector.tensor_tensor(op_lo[:, k, :], mix[:, MIX_ORDER[k], :], f32(op_hi[:, k, :]), ALU.subtract)\
                    .then_inc(op_rdy, 1)

            for c in range(3, C_OUT):
                dve.wait_ge(chunk_done, c + 1)
                if c == C_OUT - 1:
                    evac(c // 2)
                    for k in range(HK, KT):
                        op_lo_tile(k)
                    split_lo(c + 4, c + 4)
                    continue
                if c % 2 and c > 5:
                    evac(c // 2)
                for kind, i in plan.get(c, ()):
                    if kind in V_KINDS:
                        post(kind, i)
                if c == OSQ_AT:
                    out_square_sum(0)
                split_lo(c + 4, c + 4)
                if c + 2 in QS_AT:
                    split_s0_lo(QS_AT.index(c + 2))
                if c == C_OUT - 2:
                    for k in range(HK):
                        op_lo_tile(k)

            def zero_sum(n_read):
                dve.wait_ge(acc_free, n_read)
                nc.vector.memset(rstd[:], 0.0).then_inc(hsq_add, 2)

            def residual(t, par, m, squares=None):
                dve.wait_ge(acc_free, t)
                nc.vector.tensor_tensor(two(trunk[:, m, :]), acc[par % 2][:, :, 0:TH], two(trunk[:, m, :]), ALU.add)\
                    .then_inc(acc_free, 1)
                if squares is not None:
                    h_base, add_base, skip = squares
                    dve.wait_ge(acc_free, t + 1)
                    dve.nop().then_inc(h_done, 1)
                    if skip:
                        return
                    dve.wait_ge(hsq_done, m + (h_base + 1))
                    dve.wait_ge(hsq_add, m + add_base)
                    nc.vector.tensor_tensor(rstd[:], rstd[:], tmp[:, par_of(m, par), :], ALU.add)\
                        .then_inc(hsq_add, 1)

            def par_of(m, par):
                return (par + 1) % 2

            def reciprocal_std(n):
                dve.wait_ge(std_done, n)
                nc.vector.reciprocal(rstd[:], rstd[:]).then_inc(rstd_ok, 1)

            zero_sum(N_IN)
            dve.wait_ge(x_back, 16 * 4)
            def out_tiles(i, tail):
                for s in range(4):
                    c = i * 4 + (C_OUT + s)
                    dve.wait_ge(chunk_done, c + 1)
                    if s % 2:
                        residual(i * 2 + (N_IN + s // 2), N_IN + s // 2, i * 2 + s // 2, NORM_2 + (False,))
                    if tail and s == 3:
                        for k in range(HK, KT):
                            op_lo_scaled(k, 2 * KT + k + 1, V_G2 + k)
                    split_lo(c + 4, C_OUT + s + 4)
                    if tail and s == 2:
                        for k in range(HK):
                            op_lo_scaled(k, 2 * KT + k + 1, V_G2 + k)

            with dve.Fori(0, KT // 2 - 1) as i:
                out_tiles(i, False)
            out_tiles(KT // 2 - 1, True)
            reciprocal_std(1)

            def group(gr, last):
                with dve.Fori(0, FG) as f:
                    for s in range(4):
                        c = gr * C_GRP + f * 4 + (C_FF + s)
                        t = gr * (C_GRP // 2) + f * 2 + (C_FF // 2 + s // 2)
                        par = C_FF // 2 + s // 2
                        dve.wait_ge(chunk_done, c + 1)
                        if s == 1:
                            dve.wait_ge(rstd_ok, 1)
                            normalised(two(tmp[:, 1, :]), acc[par % 2])
                        if s == 3:
                            normalised(two(tmp[:, 0, :]), acc[par % 2])
                            dve.wait_ge(acc_free, t + 1)
                            dve.wait_ge(gate_act, gr * FG + f + 1)
                            nc.vector.tensor_tensor(tmp[:, 0, :], tmp[:, 0, :], tmp[:, 1, :], ALU.mult)\
                                .then_inc(hid_f, 1)
                            dve.wait_ge(hid_h, gr * FG + f + 1)
                            nc.vector.tensor_tensor(hid_lo[:, f, :], tmp[:, 0, :], f32(hid_hi[:, f, :]),
                                                    ALU.subtract).then_inc(hid_rdy, 1)
                        split_lo(c + 4, C_FF + s + 4)

                def down(i, tail):
                    for s in range(4):
                        c = gr * C_GRP + i * 4 + (C_FF + C_GU + s)
                        dve.wait_ge(chunk_done, c + 1)
                        if s % 2:
                            t0 = (C_FF + C_GU) // 2 + s // 2
                            residual(gr * (C_GRP // 2) + i * 2 + t0, t0, i * 2 + s // 2,
                                     NORM_F + (tail and s == 3,) if last else None)
                        if not tail:
                            split_lo(c + 4, C_FF + s + 4)

                if last:
                    zero_sum(gr * (C_GRP // 2) + (C_FF + C_GU) // 2)
                with dve.Fori(0, KT // 2 - (1 if last else 0)) as i:
                    down(i, False)
                if last:
                    down(KT // 2 - 1, True)

            with dve.Fori(0, GROUPS - 1) as gr:
                group(gr, False)
            group(GROUPS - 1, True)
            dve.wait_ge(var_done, 2)
            n = len(BLOCKS)
            chain(nc.vector.tensor_copy(colf, g01[:, 0, 0:n]))
            nc.vector.tensor_tensor(colf, g01[:, 1, 0:n], colf, ALU.add).then_inc(var_col, 1)
            dve.wait_ge(std_col, 1)
            chain(nc.vector.reciprocal(colf, colf))
            for a in range(2):
                js = slice(3 * a, 3 * a + 3)
                nc.vector.tensor_tensor(diag.rearrange("p (j t) -> p j t", j=n)[:, js, :],
                                        idn[:].unsqueeze(1).to_broadcast([P, 3, P]),
                                        colf[:, js].unsqueeze(2).to_broadcast([P, 3, P]), ALU.mult)\
                    .then_inc(diagonals, 1)
            dve.wait_ge(y_scaled, KT)
            for a in range(2):
                dve.wait_ge(factor_psum, a + 1)
                for k in range(2):
                    y = trunk[:, k, a * TH:(a + 1) * TH]
                    nc.vector.tensor_tensor(y, y, g23[:, a, 0:TH], ALU.mult).then_inc(out_v, 1)
            for k in range(2, NV_OUT):
                nc.vector.tensor_tensor(two(trunk[:, k, :]), two(trunk[:, k, :]), g23[:, :, 0:TH], ALU.mult)\
                    .then_inc(out_v, 1)


INS = ("xT", "w_alr", "w_in", "w_out", "w_gu", "w_da", "w_db", "vecs", "wa2", "wm", "wsbd", "bs", "s0", "cbuf",
       "ident", "tri", "maskA", "maskS", "bmask")
OUTS = (("yT", (P, KT, T)), ("gla_p", (HEADS, DK, DV)), ("gla_s", (HEADS, 2, P, 4 * DV)),
        ("conv_o", (P, 4, 2 + 2 * DB)), ("cmv", (P, 4, TS)))


def kernel(**inputs):
    import numpy as np
    import concourse.bacc as bacc
    from concourse.bass_utils import run_bass_kernel_spmd

    a = {k: np.asarray(x) for k, x in inputs.items()}

    def feature_major(x):
        return x.reshape(x.shape[0], -1, P).transpose(2, 1, 0)

    def tiles(w):
        k, m = w.shape
        return w.reshape(2, k // P // 2, P, m // P, P).transpose(3, 0, 2, 1, 4).reshape(m // P * 2, P, -1)

    x = np.concatenate([a["x_prompt"].reshape(TP, D), a["x_sample"].reshape(TS, D)])
    w = a["w_in"][0]
    parts, at = [], 0
    for n in (HEADS * DK, HEADS * DK, HEADS * DV, HEADS * DV, RANK, 512, 512, 512, 512, 512):
        parts.append(w[:, at:at + n])
        at += n
    wq, wk, wv, wr, wal, wcb, wcc, wch, wcu, wcv = parts
    conv = np.concatenate([y[:, i * P:(i + 1) * P] for i in range(4) for y in (wcc, wch, wcb)], axis=1)
    win = tiles(np.concatenate([wq, wk, wcv, wcu, wv, conv, wr], axis=1))
    wo = a["w_out"][0].reshape(KT, P, D)[MIX_ORDER].reshape(D, D)
    gu = np.stack([a["w_gate"][0].reshape(D, FT, P), a["w_up"][0].reshape(D, FT, P)], axis=2).reshape(D, 2 * DFF)
    wd = a["w_down"][0].reshape(GROUPS, FG, P, KT, P).transpose(0, 3, 2, 1, 4)
    cols = [feature_major(a[n].reshape(-1, size))[:, :, j] for n, size in
            (("norm1_g", D), ("norm2_g", D), ("final_g", D), ("gla_g", HEADS * DV), ("conv_w", 512), ("conv_b", 512),
             ("cm_ln_g", 512), ("cm_ln_b", 512)) for j in range(a[n].size // size)]
    ws = a["cm_ws"][0]
    wsbd = np.zeros((TS, 4, TS), ws.dtype)
    for b in range(DB):
        wsbd[b * DS:(b + 1) * DS, :, b * DS:(b + 1) * DS] = ws[:, :DS, :DS].transpose(2, 0, 1)
    s, t = np.arange(P)[:, None], np.arange(P)[None, :]
    tri = ((s <= t) & (s // CHUNK == t // CHUNK)) / 16.0
    tri_s = ((s <= t) & (s // DS == t // DS))[:, :TS] / 16.0
    arrays = {
        "xT": feature_major(x),
        "w_alr": wal.reshape(KT, P, RANK).transpose(1, 0, 2),
        "w_in": win,
        "w_out": tiles(wo),
        "w_gu": tiles(gu),
        "w_da": wd[:, :, :, :DA].reshape(GROUPS * KT, P, DA * P),
        "w_db": wd[:, :, :, DA:].reshape(GROUPS * KT, P, (FG - DA) * P),
        "vecs": np.concatenate(cols, axis=1),
        "wa2": np.concatenate([a["w_a2"][0], a["w_a2"][0], a["b_a"][:1]]),
        "wm": ws.transpose(2, 0, 1).reshape(P, 4 * P),
        "wsbd": wsbd,
        "bs": a["cm_bs"][0].reshape(4 * P),
        "s0": a["state_gla"][0].reshape(2, 4, HEADS, DK, DV).transpose(2, 0, 3, 1, 4).reshape(HEADS, 2, P, 4 * DV),
        "cbuf": a["state_conv"][0].reshape(2 * DB, 4, P).transpose(2, 1, 0),
        "ident": np.eye(P, dtype=np.float32),
        "tri": np.concatenate([tri, tri_s], axis=1).astype(np.float32),
        "maskA": np.tile(s % CHUNK <= t[:, :CHUNK], (1, HEADS)).astype(np.int32),
        "maskS": np.tile(((s <= t) & (s // DS == t // DS))[:TS, :TS], (1, HEADS)).astype(np.int32),
        "bmask": (s % TS // DS == t[:, :DB]).astype(np.float32),
    }
    arrays = {n: np.ascontiguousarray(y) for n, y in arrays.items()}
    nc = bacc.Bacc("TRN2", target_bir_lowering=False, num_devices=1, dynamic_dma_scratch_size=1024)
    args = [nc.dram_tensor(n, arrays[n].shape, mybir.dt.from_np(arrays[n].dtype), kind="ExternalInput").ap()
            for n in INS]
    args += [nc.dram_tensor(n, shape, F32, kind="ExternalOutput").ap() for n, shape in OUTS]
    build(nc, *args)
    r = run_bass_kernel_spmd(nc, [arrays], core_ids=[0]).results[0]
    y = r["yT"].transpose(2, 1, 0).reshape(T, D)
    cst = r["conv_o"].transpose(2, 1, 0).reshape(2 + 2 * DB, 512)
    gs = r["gla_s"].reshape(HEADS, 2, DK, 4, DV).transpose(1, 3, 0, 2, 4).reshape(1, DB, HEADS, DK, DV)
    return (y[:TP].reshape(1, TP, D), y[TP:].reshape(DB, DS, D), r["gla_p"].reshape(1, 1, HEADS, DK, DV),
            cst[:2].reshape(1, 1, 2, 512), gs, cst[2:].reshape(1, DB, 2, 512),
            r["cmv"].transpose(2, 1, 0).reshape(1, DB, DS, 512))
```
